# Optimizing a Trainium2 kernel written in Bass

```python
import jax, jax.numpy as jnp
from jax import lax
import numpy as np

D_MODEL = 1024
BATCH = 1
SEQ = 512
DEPTH = 2

CTX_LEN = 256
GRID_W = 64
D_MIX = D_MODEL
D_HGRN = D_MIX // 2
HGRN_HEADS = 4
HGRN_DH = D_HGRN // HGRN_HEADS
D_RWKV = D_MIX - D_HGRN
RWKV_DH = 64
RWKV_HEADS = D_RWKV // RWKV_DH
W_RANK = 64
A_RANK = 64
G_RANK = 128
D_FF = ((8 * D_MODEL // 3 + 255) // 256) * 256
CHUNK = 64
N_MOD = 9
RMS_EPS = 1e-6
GN_EPS = 64e-5
HG_COLS = 5 * D_HGRN
RW_COLS = 3 * D_RWKV + 2 * W_RANK + 2 * A_RANK + G_RANK
N_IN = HG_COLS + RW_COLS
RW_SPLITS = (D_RWKV, 2 * D_RWKV, 3 * D_RWKV, 3 * D_RWKV + W_RANK, 3 * D_RWKV + 2 * W_RANK,
             3 * D_RWKV + 2 * W_RANK + A_RANK, 3 * D_RWKV + 2 * W_RANK + 2 * A_RANK)

kernel_name = 'hybrid_hgrn2_rwkv7_prefix_dit'

def rms_norm(x, gain):
    xf = x.astype(jnp.float32)
    y = xf * lax.rsqrt(jnp.mean(xf * xf, axis=-1, keepdims=True) + RMS_EPS)
    return (y * gain.astype(jnp.float32)).astype(x.dtype)

def modulate(h, shift, scale):
    return h * (1 + scale) + shift

def swiglu(h, w_up, w_down):
    gate, up = jnp.split(h @ w_up, 2, axis=-1)
    return (jax.nn.silu(gate) * up) @ w_down

def ffn_half_step(x, gain, shift, scale, gate, w_up, w_down):
    h = modulate(rms_norm(x, gain), shift, scale)
    return x + 0.5 * gate * swiglu(h, w_up, w_down)

def grid_conv(u, kern):
    b, length, ch = u.shape
    img = u.reshape(b, length // GRID_W, GRID_W, ch)
    out = lax.conv_general_dilated(img, kern[:, :, None, :].astype(u.dtype), (1, 1), 'SAME',
                                   dimension_numbers=('NHWC', 'HWIO', 'NHWC'), feature_group_count=ch)
    return out.reshape(b, length, ch)

def seq_conv(u, taps):
    up = jnp.pad(u, ((0, 0), (1, 1), (0, 0)))
    return up[:, :-2] * taps[0] + up[:, 1:-1] * taps[1] + up[:, 2:] * taps[2]

def flip_segments(u, n_ctx):
    return jnp.concatenate([jnp.flip(u[:, :n_ctx], 1), jnp.flip(u[:, n_ctx:], 1)], axis=1)

def split_heads(u, n_heads):
    n, t, _ = u.shape
    return u.reshape(n, t, n_heads, -1).transpose(0, 2, 1, 3)

def merge_heads(u):
    n, h, t, d = u.shape
    return u.transpose(0, 2, 1, 3).reshape(n, t, h * d)

def head_rms_norm(o, gain, n_heads):
    shp = o.shape
    oh = o.reshape(*shp[:-1], n_heads, -1)
    oh = oh * lax.rsqrt(jnp.mean(oh * oh, axis=-1, keepdims=True) + RMS_EPS)
    return oh.reshape(shp) * gain

def head_group_norm(y, w, b, n_heads):
    shp = y.shape
    yh = y.reshape(*shp[:-1], n_heads, -1)
    mu = jnp.mean(yh, axis=-1, keepdims=True)
    var = jnp.mean(jnp.square(yh - mu), axis=-1, keepdims=True)
    yh = (yh - mu) * lax.rsqrt(var + GN_EPS)
    return yh.reshape(shp) * w + b

def hgrn_forget(z, lb):
    log_f = jnp.logaddexp(jnp.log(lb), jnp.log1p(-lb) + jax.nn.log_sigmoid(z))
    key = (1.0 - lb) * jax.nn.sigmoid(-z)
    return log_f, key

def gla_chunk_scan(q, k, v, log_f):
    n, h, t, dk = q.shape
    dv = v.shape[-1]
    nc = t // CHUNK
    def chunks(u):
        return jnp.moveaxis(u.reshape(n, h, nc, CHUNK, u.shape[-1]), 2, 0)
    causal = jnp.tril(jnp.ones((CHUNK, CHUNK), dtype=bool))[:, :, None]
    def step(state, inp):
        qc, kc, vc, gc = inp
        b = jnp.cumsum(gc, axis=2)
        diff = b[:, :, :, None, :] - b[:, :, None, :, :]
        decay = jnp.exp(jnp.where(causal, diff, -jnp.inf))
        att = jnp.einsum('nhtd,nhsd,nhtsd->nhts', qc, kc, decay)
        out = (jnp.einsum('nhts,nhsv->nhtv', att, vc)
               + jnp.einsum('nhtd,nhdv->nhtv', qc * jnp.exp(b), state))
        b_last = b[:, :, -1:, :]
        state = (state * jnp.exp(b_last)[:, :, 0, :, None]
                 + jnp.einsum('nhsd,nhsv->nhdv', kc * jnp.exp(b_last - b), vc))
        return state, out
    s0 = jnp.zeros((n, h, dk, dv), jnp.float32)
    _, o = lax.scan(step, s0, (chunks(q), chunks(k), chunks(v), chunks(log_f)))
    return jnp.moveaxis(o, 0, 2).reshape(n, h, t, dv)

def rwkv7_scan(r, w, k, v, kk, a):
    n, h, d = r.shape[1:]
    def step(state, inp):
        r_t, w_t, k_t, v_t, kk_t, a_t = inp
        sa = jnp.einsum('nhvk,nhk->nhv', state, -kk_t)
        state = (state * w_t[:, :, None, :] + sa[..., None] * (kk_t * a_t)[:, :, None, :]
                 + v_t[..., None] * k_t[:, :, None, :])
        return state, jnp.einsum('nhvk,nhk->nhv', state, r_t)
    s0 = jnp.zeros((n, h, d, d), jnp.float32)
    _, y = lax.scan(step, s0, (r, w, k, v, kk, a))
    return y

def rwkv_decay(wd, w0, w_up):
    w = -jax.nn.softplus(-(w0 + jnp.tanh(wd) @ w_up)) - 0.5
    return jnp.exp(-jnp.exp(w))

def token_mix(hx, hc, w_in, w_out, lb, o_gain, conv, w0, w_up, a0, a_up, g_up,
              k_k, k_a, r_k, ln_w, ln_b, with_ctx_out):
    bsz = hx.shape[0]
    n_ctx = hc.shape[1]
    f32 = jnp.float32
    px = hx @ w_in
    pc = hc @ w_in
    rw_x = grid_conv(px[..., HG_COLS:], conv)
    rw_c = seq_conv(pc[..., HG_COLS:], conv[1])
    hg = jnp.concatenate([pc[..., :HG_COLS], px[..., :HG_COLS]], axis=1).astype(f32)
    rw = jnp.concatenate([rw_c, rw_x], axis=1).astype(f32)
    t_len = hg.shape[1]
    rev = lambda u: flip_segments(u, n_ctx)
    both = lambda fw, bw: jnp.concatenate([fw, rev(bw)], axis=0)

    q, zf_fw, zf_bw, i_in, g_out = jnp.split(hg, 5, axis=-1)
    q = jax.nn.silu(q)
    lf_fw, k_fw = hgrn_forget(zf_fw, lb[0])
    lf_bw, k_bw = hgrn_forget(zf_bw, lb[1])
    o = gla_chunk_scan(split_heads(both(q, q), HGRN_HEADS), split_heads(both(k_fw, k_bw), HGRN_HEADS),
                       split_heads(both(i_in, i_in), HGRN_HEADS), split_heads(both(lf_fw, lf_bw), HGRN_HEADS))
    o = merge_heads(o)
    o = o[:bsz] + rev(o[bsz:])
    o = head_rms_norm(o, o_gain, HGRN_HEADS) * jax.nn.silu(g_out)

    r, k, v, wd_fw, wd_bw, ad_fw, ad_bw, gd = jnp.split(rw, RW_SPLITS, axis=-1)
    dec_fw = rwkv_decay(wd_fw, w0[0], w_up[0])
    dec_bw = rwkv_decay(wd_bw, w0[1], w_up[1])
    a_fw = jax.nn.sigmoid(a0[0] + ad_fw @ a_up[0])
    a_bw = jax.nn.sigmoid(a0[1] + ad_bw @ a_up[1])
    g_r = jax.nn.sigmoid(gd) @ g_up
    kk = (k * k_k).reshape(bsz, t_len, RWKV_HEADS, RWKV_DH)
    kk = kk / jnp.maximum(jnp.linalg.norm(kk, axis=-1, keepdims=True), 1e-12)
    kk = kk.reshape(bsz, t_len, D_RWKV)
    kf = k * (1 + (a_fw - 1) * k_a)
    kb = k * (1 + (a_bw - 1) * k_a)
    tm = lambda u: split_heads(u, RWKV_HEADS).transpose(2, 0, 1, 3)
    y = rwkv7_scan(tm(both(r, r)), tm(both(dec_fw, dec_bw)), tm(both(kf, kb)),
                   tm(both(v, v)), tm(both(kk, kk)), tm(both(a_fw, a_bw)))
    y = merge_heads(y.transpose(1, 2, 0, 3))
    y = y[:bsz] + rev(y[bsz:])
    y = head_group_norm(y, ln_w, ln_b, RWKV_HEADS)
    bonus = (jnp.sum((r * (kf + kb)).reshape(bsz, t_len, RWKV_HEADS, RWKV_DH) * r_k, axis=-1, keepdims=True)
             * v.reshape(bsz, t_len, RWKV_HEADS, RWKV_DH))
    y = (y + bonus.reshape(bsz, t_len, D_RWKV)) * g_r

    mixed = jnp.concatenate([o, y], axis=-1).astype(hx.dtype)
    out_x = mixed[:, n_ctx:] @ w_out
    out_c = mixed[:, :n_ctx] @ w_out if with_ctx_out else None
    return out_x, out_c

def setup_inputs(seed: int = 0) -> dict:
    key = jax.random.key(seed)
    ks = iter(jax.random.split(key, 32))
    nrm = lambda shape, s: s * jax.random.normal(next(ks), shape, jnp.float32)
    D = D_MODEL
    x = nrm((BATCH, SEQ, D), 1.0)
    c = nrm((BATCH, D), 1.0)
    ctx = nrm((BATCH, CTX_LEN, D), 1.0)
    c_ctx = nrm((D,), 1.0)
    w_mod = nrm((DEPTH, D, N_MOD * D), 0.5 * D ** -0.5)
    b_mod = nrm((DEPTH, N_MOD * D), 0.01)
    norm_gains = 1.0 + nrm((DEPTH, 3, D), 0.05)
    final_gain = 1.0 + nrm((D,), 0.05)
    ffn1_up = nrm((DEPTH, D, 2 * D_FF), D ** -0.5)
    ffn1_down = nrm((DEPTH, D_FF, D), D_FF ** -0.5)
    ffn2_up = nrm((DEPTH, D, 2 * D_FF), D ** -0.5)
    ffn2_down = nrm((DEPTH, D_FF, D), D_FF ** -0.5)
    w_in = nrm((DEPTH, D, N_IN), D ** -0.5)
    w_out = nrm((DEPTH, D_MIX, D), D_MIX ** -0.5)
    hgrn_lb_logits = nrm((DEPTH, 2, D_HGRN), 1.0)
    hgrn_o_gain = 1.0 + nrm((DEPTH, D_HGRN), 0.05)
    rwkv_conv = nrm((DEPTH, 3, 3, RW_COLS), 0.1).at[:, 1, 1].add(1.0)
    rwkv_w0 = jax.random.uniform(next(ks), (DEPTH, 2, D_RWKV), jnp.float32, -6.0, 0.0)
    rwkv_w_up = nrm((DEPTH, 2, W_RANK, D_RWKV), 0.1 * W_RANK ** -0.5)
    rwkv_a0 = nrm((DEPTH, 2, D_RWKV), 0.1)
    rwkv_a_up = nrm((DEPTH, 2, A_RANK, D_RWKV), 0.1 * A_RANK ** -0.5)
    rwkv_g_up = nrm((DEPTH, G_RANK, D_RWKV), G_RANK ** -0.5)
    rwkv_k_k = 0.85 + nrm((DEPTH, D_RWKV), 0.05)
    rwkv_k_a = 1.0 + nrm((DEPTH, D_RWKV), 0.05)
    rwkv_r_k = nrm((DEPTH, RWKV_HEADS, RWKV_DH), 0.1)
    rwkv_ln_w = 1.0 + nrm((DEPTH, D_RWKV), 0.05)
    rwkv_ln_b = nrm((DEPTH, D_RWKV), 0.01)
    return {'x': x, 'c': c, 'ctx': ctx, 'c_ctx': c_ctx, 'w_mod': w_mod, 'b_mod': b_mod,
            'norm_gains': norm_gains, 'final_gain': final_gain,
            'ffn1_up': ffn1_up, 'ffn1_down': ffn1_down, 'ffn2_up': ffn2_up, 'ffn2_down': ffn2_down,
            'w_in': w_in, 'w_out': w_out, 'hgrn_lb_logits': hgrn_lb_logits, 'hgrn_o_gain': hgrn_o_gain,
            'rwkv_conv': rwkv_conv, 'rwkv_w0': rwkv_w0, 'rwkv_w_up': rwkv_w_up, 'rwkv_a0': rwkv_a0,
            'rwkv_a_up': rwkv_a_up, 'rwkv_g_up': rwkv_g_up, 'rwkv_k_k': rwkv_k_k, 'rwkv_k_a': rwkv_k_a,
            'rwkv_r_k': rwkv_r_k, 'rwkv_ln_w': rwkv_ln_w, 'rwkv_ln_b': rwkv_ln_b}

def reference(x, c, ctx, c_ctx, w_mod, b_mod, norm_gains, final_gain, ffn1_up, ffn1_down, ffn2_up,
              ffn2_down, w_in, w_out, hgrn_lb_logits, hgrn_o_gain, rwkv_conv, rwkv_w0, rwkv_w_up,
              rwkv_a0, rwkv_a_up, rwkv_g_up, rwkv_k_k, rwkv_k_a, rwkv_r_k, rwkv_ln_w, rwkv_ln_b):
    p = jax.nn.softmax(hgrn_lb_logits.astype(jnp.float32), axis=0)
    cum = jnp.cumsum(p, axis=0)
    lower_bounds = cum - cum[0]
    sc = jax.nn.silu(c)
    scc = jax.nn.silu(c_ctx)
    for l in range(DEPTH):
        last = l == DEPTH - 1
        mx = jnp.split((sc @ w_mod[l] + b_mod[l])[:, None, :], N_MOD, axis=-1)
        mc = jnp.split(scc @ w_mod[l] + b_mod[l], N_MOD, axis=-1)
        x = ffn_half_step(x, norm_gains[l, 0], mx[0], mx[1], mx[2], ffn1_up[l], ffn1_down[l])
        ctx = ffn_half_step(ctx, norm_gains[l, 0], mc[0], mc[1], mc[2], ffn1_up[l], ffn1_down[l])
        hx = modulate(rms_norm(x, norm_gains[l, 1]), mx[3], mx[4])
        hc = modulate(rms_norm(ctx, norm_gains[l, 1]), mc[3], mc[4])
        mix_x, mix_c = token_mix(hx, hc, w_in[l], w_out[l], lower_bounds[l], hgrn_o_gain[l], rwkv_conv[l],
                                 rwkv_w0[l], rwkv_w_up[l], rwkv_a0[l], rwkv_a_up[l], rwkv_g_up[l],
                                 rwkv_k_k[l], rwkv_k_a[l], rwkv_r_k[l], rwkv_ln_w[l], rwkv_ln_b[l],
                                 not last)
        x = x + mx[5] * mix_x
        x = ffn_half_step(x, norm_gains[l, 2], mx[6], mx[7], mx[8], ffn2_up[l], ffn2_down[l])
        if not last:
            ctx = ctx + mc[5] * mix_c
            ctx = ffn_half_step(ctx, norm_gains[l, 2], mc[6], mc[7], mc[8], ffn2_up[l], ffn2_down[l])
    return rms_norm(x, final_gain)


_drawn_inputs = setup_inputs


def setup_inputs(seed=0):
    import zlib

    import numpy as np

    out = dict(_drawn_inputs(seed))
    spreads = {}
    factors = {'b_mod': 3.64,
     'hgrn_lb_logits': 6.37,
     'hgrn_o_gain': 5.576,
     'rwkv_w_up': 8.0,
     'rwkv_a0': 6.521,
     'rwkv_a_up': 4.943,
     'rwkv_k_k': 4.882,
     'rwkv_k_a': 3.893,
     'rwkv_ln_w': 6.293,
     'rwkv_ln_b': 37.675}
    for name, (base, spread) in spreads.items():
        noise = np.random.default_rng([zlib.crc32(name.encode()), seed]).standard_normal(out[name].shape)
        drawn = base * np.exp(spread * noise) if base else spread * noise
        out[name] = __import__('jax').numpy.asarray(drawn.astype(out[name].dtype))
    for name, factor in factors.items():
        out[name] = (out[name] * factor).astype(out[name].dtype)
    return out
```

```python
from contextlib import ExitStack

import concourse.bass as bass
from concourse import mybir

F32 = mybir.dt.float32
U32 = mybir.dt.uint32
ALU = mybir.AluOpType
ACT = mybir.ActivationFunctionType

P = 128
DEPTH = 2
D = 1024
KT = D // P
CTX, LAT = 256, 512
T = CTX + LAT
GRID_W = 64
GRID_H = LAT // GRID_W
F = 2816
FT = F // P
HT = 4
N_MOD = 9
MT = N_MOD * KT
HG_T = 5 * HT
RW_T = 15
RMS_EPS, GN_EPS = 1e-6, 64e-5
RSQRT_E = 0.6065306597126334
NEVER = -1e30

RING = 4
S_MOD, S_UP1 = 0, MT
S_DN1 = S_UP1 + 2 * FT
S_HG = S_DN1 + 3 * KT
S_RW = S_HG + HG_T
S_OUT = S_RW + RW_T + 1
S_UP2 = S_OUT + KT
S_DN2 = S_UP2 + 2 * FT
SLOTS = S_DN2 + 3 * KT
assert all(s % RING == 0 for s in (S_UP1, S_DN1, S_HG, S_RW, S_OUT, S_UP2, S_DN2, SLOTS))
DOWN_K = (8, 8, FT - 16)

COLS = {}
_n = 0
for _name, _w in (("gain", 3 * KT), ("ogain", HT), ("taps", RW_T * 9), ("w0", 2 * HT), ("a0", 2 * HT),
                  ("k_k", HT), ("k_a", HT), ("r_k", HT), ("ln_w", HT), ("ln_b", HT), ("b_mod", MT)):
    COLS[_name] = (_n, _n + _w)
    _n += _w
NPAR = _n

GC = 128
GN = T // GC
LEVELS = [64, 32, 16, 8, 4, 2, 1]
RC = 64
RN = T // RC
RN_CTX = CTX // RC
INV = [1, 2, 4, 8, 16, 32]
GLA_ORDER = {0: [0, 1, 2, 3, 4, 5], 1: [1, 0, 5, 4, 3, 2]}

C_ID, C_ONE, C_BLK = 0, P, 2 * P
C_LVL = 3 * P
C_AM = C_LVL + 2 * len(LEVELS) * P
C_INV = C_AM + 2 * P
C_INV0T = C_INV + len(INV) * P
C_FG = C_INV0T + P
NCST = C_FG + KT


def ordered(engine, instruction):
    def issue(*args, **kwargs):
        made = instruction(*args, **kwargs)
        engine.drain()
        return made
    return issue


def build_program(nc, x_in, wstream, par_in, small_in, cst_in, logit_in, cvec_in, out):
    o_spill = nc.dram_tensor("o_spill", (P, HT, T), F32, kind="Internal").ap()
    spill = nc.dram_tensor("x_spill", (P, KT, T), F32, kind="Internal").ap()
    ctx = ExitStack()
    with ctx:
        def sb(name, cols):
            return ctx.enter_context(nc.sbuf_tensor(name, [P, cols], F32))

        def sem(name):
            return ctx.enter_context(nc.semaphore(name))

        ps = ctx.enter_context(nc.psum_tensor("ps", [P, 8, 512], F32))
        XR = sb("XR", KT * T)
        HR = sb("HR", KT * T)
        MIX = sb("MIX", KT * T)
        AR = sb("AR", 27 * T)
        WR = sb("WR", RING * 1024)
        TMP = sb("TMP", 4096)
        CST = sb("CST", NCST)
        PAR = sb("PAR", NPAR)
        SMALL = sb("SMALL", 3 * 512)
        MOD = sb("MOD", MT * 2)
        COEF = sb("COEF", 9 * KT * 2)
        MTMP = sb("MTMP", RING * 2)
        LG = sb("LG", 8 * 8)
        LBC = sb("LBC", DEPTH * 16)
        LBH = sb("LBH", 4)
        KAX = sb("KAX", 2 * HT)
        EBL = sb("EBL", GN)
        PCT = sb("PCT", 2 * HT)
        EPS = sb("EPS", 2)
        eps_rms, eps_gn = EPS[:, 0:1], EPS[:, 1:2]

        X = XR[:, :].rearrange("p (k t) -> p k t", k=KT)
        H = HR[:, :].rearrange("p (k t) -> p k t", k=KT)
        MX = MIX[:, :].rearrange("p (k t) -> p k t", k=KT)
        A = AR[:, :].rearrange("p (k t) -> p k t", t=T)
        W = [WR[:, j * 1024:(j + 1) * 1024] for j in range(RING)]
        TM = TMP[:, 0:5 * T].rearrange("p (k t) -> p k t", t=T)
        ident = CST[:, C_ID:C_ID + P]
        ones = CST[:, C_ONE:C_ONE + P]
        blk = CST[:, C_BLK:C_BLK + P]
        modv = MOD[:, :].rearrange("p (n k s) -> p n k s", n=N_MOD, s=2)
        coef = COEF[:, :].rearrange("p (n q k s) -> p n q k s", n=3, q=3, s=2)
        CBC = AR[:, 0:2048].rearrange("p (s k) -> p s k", s=2)
        JUNK = AR[:, 2048:4096].rearrange("p (s k) -> p s k", s=2)

        def par(name, i, n=1):
            a, _ = COLS[name]
            return PAR[:, a + i:a + i + n]

        cst_in_sem = sem("cst_loaded")
        x_loaded = sem("x_loaded")
        par_loaded = sem("par_loaded")
        w_ready = [sem(f"w_ready{j}") for j in range(RING)]
        w_used = sem("w_used")
        dve_setup = sem("dve_setup")
        act_setup = sem("act_setup")
        cvec_loaded = sem("cvec_loaded")
        cvec_ready = sem("cvec_ready")
        layer_done_dve = sem("layer_done_dve")
        layer_done_act = sem("layer_done_act")
        mod_done = sem("mod_done")
        spilled = sem("x_spilled")
        reloaded = sem("x_reloaded")
        xr_free = sem("xr_free")
        out_sem = sem("out_stored")

        class NormSems:
            def __init__(s, n):
                s.sq_ready = sem(f"{n}_sq_ready")
                s.sq_used = sem(f"{n}_sq_used")
                s.std_ready = sem(f"{n}_std_ready")
                s.h_ready = sem(f"{n}_h_ready")

        norms = [NormSems(f"norm{i}") for i in range(3)]
        fnorm = NormSems("final")

        class FfnSems:
            def __init__(s, n):
                s.silu_done = sem(f"{n}_silu_done")
                s.act_done = sem(f"{n}_act_done")
                s.res_done = sem(f"{n}_res_done")

        ffns = [FfnSems("ffn1"), FfnSems("ffn2")]
        hg_ev = sem("hg_ev")
        hg_silu = sem("hg_silu")
        rw_ev = sem("rw_ev")
        rw_conv = sem("rw_conv")
        out_res = sem("out_res")

        g_in = sem("gla_in")
        g_vt_ps = sem("gla_vt_ps")
        g_vt = sem("gla_vt")
        g_lb = sem("gla_lb")
        g_gate = sem("gla_gate")
        g_w = sem("gla_w")
        g_kx = sem("gla_kx")
        g_k = sem("gla_k")
        g_qe = sem("gla_qe")
        g_ke = sem("gla_ke")
        g_kt_ps = sem("gla_kt_ps")
        g_kt = sem("gla_kt")
        g_u = sem("gla_u")
        g_s = sem("gla_s")
        g_dx = sem("gla_dx")
        g_ex = sem("gla_ex")
        g_z = sem("gla_z")
        g_att_ps = sem("gla_att_ps")
        g_att = sem("gla_att")
        g_o_ps = sem("gla_o_ps")
        g_o = sem("gla_o")
        on_sq = sem("on_sq")
        on_ps = sem("on_ps")
        on_std = sem("on_std")
        on_done = sem("on_done")

        p_th = sem("rp_tanh")
        p_mm = sem("rp_mm")
        p_ev = sem("rp_ev")
        p_lw = sem("rp_lw")
        p_kk = sem("rp_kk")
        p_sq = sem("rp_sq")
        p_ss = sem("rp_ss")
        p_mx = sem("rp_mx")
        p_sd = sem("rp_sd")
        p_kn = sem("rp_kn")

        r_cum = sem("rk_cum")
        r_exp = sem("rk_exp")
        r_bk = sem("rk_bk")
        r_kr = sem("rk_kr")
        r_tv = sem("rk_tv")
        r_tve = sem("rk_tve")
        r_am_ps = sem("rk_am_ps")
        r_am = sem("rk_am")
        r_r = sem("rk_r")
        r_re = sem("rk_re")
        r_t = sem("rk_t")
        r_w = sem("rk_w")
        r_xy = sem("rk_xy")
        r_xye = sem("rk_xye")
        r_sa = sem("rk_sa")
        r_sae = sem("rk_sae")
        r_s = sem("rk_s")
        r_y = sem("rk_y")
        r_ye = sem("rk_ye")
        o_spilled = sem("o_spilled")
        q_std = sem("rq_std")
        q_a = sem("rq_a")
        q_b = sem("rq_b")
        q_c = sem("rq_c")
        q_d = sem("rq_d")
        q_e = sem("rq_e")
        q_f = sem("rq_f")

        def slot_value(l, s, extra=0):
            return (l * (SLOTS // RING) + s // RING + extra + 1) * 16

        def halves(b):
            return ((slice(0, CTX), ps[:, b, 0:CTX]), (slice(CTX, T), ps[:, b + 1, 0:LAT]))

        def xt(i):
            return XR[:, i * T:(i + 1) * T]

        G_QS, G_KS, G_B, G_IS, G_VT, G_KET, G_KE = xt(0), xt(1), xt(2), xt(3), xt(4), xt(5), xt(6)
        G_QE = [A[:, 20], A[:, 21]]
        G_ATT = [A[:, 22], A[:, 23]]
        G_S = [A[:, 24], A[:, 25]]
        G_E = [TM[:, 0], TM[:, 1]]
        G_Z = [TM[:, 2], TM[:, 3]]

        at = [0]

        def rb(n):
            a = at[0]
            at[0] += n
            assert at[0] <= KT * T
            return XR[:, a:a + n]

        R_UI = rb(1024).rearrange("p (h c) -> p h c", h=8)
        R_AKK = rb(1024).rearrange("p (h c) -> p h c", h=8)
        R_AMR = rb(1024).rearrange("p (d h c) -> p d h c", d=2, h=8)
        R_BKT = rb(1024).rearrange("p (d j c) -> p d j c", d=2, j=HT)
        R_SAV = rb(1024).rearrange("p (d h c) -> p d h c", d=2, h=8)
        R_STF = rb(1024)
        R_ST = R_STF.rearrange("p (d j c) -> p d j c", d=2, j=HT)

        R_KR = TMP[:, 0:1024].rearrange("p (d j a c) -> p d j a c", d=2, j=HT, a=2)
        R_BK = TMP[:, 1024:2048].rearrange("p (d j a c) -> p d j a c", d=2, j=HT, a=2)
        R_X = TMP[:, 2048:3072].rearrange("p (h c) -> p h c", h=8)
        R_Y = TMP[:, 3072:4096].rearrange("p (h c) -> p h c", h=8)
        R_W = AR[:, 12 * T:12 * T + 1024].rearrange("p (h c) -> p h c", h=8)
        R_RS = AR[:, 12 * T + 1024:14 * T].rearrange("p (h c) -> p h c", h=8)
        R_EI = SMALL[:, 0:512].rearrange("p (d j c) -> p d j c", d=2, j=HT)
        R_T1 = SMALL[:, 512:1024].rearrange("p (d j c) -> p d j c", d=2, j=HT)
        R_EP = MIX[:, 0:2 * HT * (RC + 1)].rearrange("p (d j c) -> p d j c", d=2, j=HT)
        R_VS = MIX[:, 1024:1536].rearrange("p (h c) -> p h c", h=8)

        R_r, R_k, R_v, R_kk = A[:, 0:4], A[:, 4:8], A[:, 8:12], A[:, 15:19]
        R_a = [A[:, 19:23], A[:, 23:27]]
        R_lw = [H[:, 0:4], H[:, 4:8]]
        YB = MX[:, HT:2 * HT]

        settled = {}

        def settle(engine, name):
            if name not in settled:
                settled[name] = sem(f"{name}_settled")
            engine.sem_inc(settled[name], 1)

        block = ctx.enter_context(nc.Block())

        @block.sync
        def _(sp):
            for j in range(RING):
                sp.dma_start(W[j], wstream[j]).then_inc(w_ready[j], 16)
            with sp.Fori(1, DEPTH * SLOTS // RING) as g:
                for j in range(RING):
                    sp.wait_ge(w_used, g * RING + (j + 1 - RING))
                    sp.dma_start(W[j], wstream[g * RING + j]).then_inc(w_ready[j], 16)
            sp.wait_ge(fnorm.h_ready, 1)
            sp.dma_start(out, H[:, :, CTX:T]).then_inc(out_sem, 16)
            sp.wait_ge(out_sem, 16)

        @block.gpsimd
        def _(pool):
            pool.dma_start(CST[:, :], cst_in).then_inc(cst_in_sem, 16)
            pool.dma_start(LG[:, 0:16], logit_in).then_inc(cst_in_sem, 16)
            pool.dma_start(X, x_in).then_inc(x_loaded, 16)
            with pool.Fori(0, DEPTH) as l:
                pool.wait_ge(layer_done_dve, l + 1)
                pool.wait_ge(layer_done_act, l + 1)
                settle(pool, "pool")
                pool.dma_start(PAR[:, :], par_in[l]).then_inc(par_loaded, 16)
                pool.dma_start(SMALL[:, :], small_in[l]).then_inc(par_loaded, 16)
                pool.dma_start(AR[:, 0:2048], cvec_in).then_inc(cvec_loaded, 16)
                pool.wait_ge(norms[1].h_ready, l + 1)
                settle(pool, "pool")
                pool.dma_start(spill, X).then_inc(spilled, 16)
                pool.wait_ge(on_done, l + 1)
                settle(pool, "pool")
                pool.dma_start(o_spill, MX[:, 0:HT]).then_inc(o_spilled, 16)
                pool.wait_ge(xr_free, l + 1)
                settle(pool, "pool")
                pool.dma_start(MX[:, 0:HT], o_spill).then_inc(reloaded, 16)
                pool.dma_start(X, spill).then_inc(reloaded, 16)

        @block.tensor
        def _(pe):
            def tile_products(b, j, rhs, k0, nk, start, stop):
                for k in range(nk):
                    for sl, dst in halves(b):
                        last = pe.matmul(dst, W[j][:, k * P:(k + 1) * P], rhs[:, k0 + k, sl],
                                         start=start and k == 0, stop=stop and k == nk - 1)
                return last

            def norm(l, s):
                for k in range(KT):
                    pe.wait_ge(s.sq_ready, l * KT + k + 1)
                    for sl, dst in halves(0):
                        last = pe.matmul(dst, ones, TM[:, k % 2, sl], start=k == 0, stop=k == KT - 1)
                    last.then_inc(s.sq_used, 1)

            def ffn(l, n, up, dn):
                s = ffns[n]
                pe.wait_ge(norms[2 * n].h_ready, l + 1)
                settle(pe, "pe")
                with pe.Fori(0, FT // 2) as i:
                    for j in range(2):
                        pe.wait_ge(s.act_done, l * FT + i * 2 + (j + 1))
                        for a in range(2):
                            pe.wait_ge(w_ready[2 * j + a], slot_value(l, up, i))
                            last = tile_products(4 * j + 2 * a, 2 * j + a, H, 0, KT, True, True)
                            last.then_inc(w_used, 1)
                pe.wait_ge(s.act_done, (l + 1) * FT + 2)
                settle(pe, "pe")
                with pe.Fori(0, 2) as g:
                    for m in range(4):
                        pe.wait_ge(s.res_done, l * KT + g * 4 + (m + 1))
                        k0 = 0
                        for r, nk in enumerate(DOWN_K):
                            t = 3 * m + r
                            pe.wait_ge(w_ready[t % RING], slot_value(l, dn + t, g * 3))
                            last = tile_products(2 * m, t % RING, A, k0, nk, r == 0, r == 2)
                            last.then_inc(w_used, 1)
                            k0 += nk

            def project(l, first, n, n4, rhs, ev):
                def group(i, k):
                    for j in range(k):
                        pe.wait_ge(ev, l * n + i * RING + (j + 1))
                        pe.wait_ge(w_ready[j], slot_value(l, first, i))
                        pad = 0
                        if j == k - 1 and k < RING:
                            pad = RING - k
                            pe.wait_ge(w_ready[RING - 1], slot_value(l, first, i))
                        last = tile_products(2 * j, j, rhs, 0, KT, True, True)
                        last.then_inc(w_used, 1 + pad)
                with pe.Fori(0, n4) as i:
                    group(i, RING)
                if n > n4 * RING:
                    group(n4, n - n4 * RING)

            def three(b, c):
                return ps[:, b + c // 3, (c % 3) * GC:(c % 3 + 1) * GC]

            def gla(l):
                pe.wait_ge(hg_silu, l + 1)
                pe.wait_ge(hg_ev, (l + 1) * HG_T + 4)
                settle(pe, "pe")
                with pe.Fori(0, HT) as h:
                    u = l * HT + h
                    pe.wait_ge(g_in, u + 1)
                    for c in range(GN):
                        last = pe.transpose(three(4, c), G_IS[:, c * GC:(c + 1) * GC], ident)
                    last.then_inc(g_vt_ps, 1)
                    pe.wait_ge(g_vt, u + 1)
                    for d in range(2):
                        v = u * 2 + (d + 1)
                        n8 = (u * 2 + d) * 8
                        pe.wait_ge(g_k, v)
                        for c in range(GN):
                            sl = slice(c * GC, (c + 1) * GC)
                            last = pe.matmul(three(0, c), G_KS[:, sl], G_QS[:, sl], start=True, stop=True)
                        last.then_inc(g_att_ps, 1)
                        pe.wait_ge(g_ke, v)
                        for c in range(GN):
                            last = pe.transpose(three(4, c), G_KE[:, c * GC:(c + 1) * GC], ident)
                        last.then_inc(g_kt_ps, 1)
                        pe.wait_ge(g_kt, v)
                        for c in range(GN):
                            sl = slice(c * GC, (c + 1) * GC)
                            last = pe.matmul(three(4, c), G_KET[:, sl], G_VT[:, sl], start=True, stop=True)
                        last.then_inc(g_u, 1)
                        for n in range(len(LEVELS)):
                            b = 2 * ((n + 1) % 2)
                            pe.wait_ge(g_z, (u * 2 + d) * 7 + (n + 1))
                            if n >= 1:
                                pe.wait_ge(g_att, n8 + n)
                            for c in range(GN):
                                sl = slice(c * GC, (c + 1) * GC)
                                z = G_Z[n % 2][:, sl]
                                last = pe.matmul(three(b, c), z, z, start=True, stop=True)
                            last.then_inc(g_att_ps, 1)
                        pe.wait_ge(g_att, n8 + 8)
                        pe.wait_ge(g_s, v)
                        for c in range(GN):
                            sl = slice(c * GC, (c + 1) * GC)
                            first = GLA_ORDER[d][0]
                            last = pe.matmul(three(6, c), G_VT[:, sl], G_ATT[d][:, sl],
                                             start=d == 0 and c % 3 == 0, stop=d == 1 and c == first,
                                             skip_group_check=True)
                            if c != first:
                                last = pe.matmul(three(6, c), G_S[d][:, sl], G_QE[d][:, sl],
                                                 start=False, stop=d == 1, skip_group_check=True)
                    last.then_inc(g_o_ps, 1)
                    pe.wait_ge(g_o, u + 1)

            def o_norm(l):
                for h in range(HT):
                    pe.wait_ge(on_sq, l * HT + h + 1)
                    for sl, dst in halves(2 * h):
                        last = pe.matmul(dst, ones, TM[:, h, sl], start=True, stop=True)
                    last.then_inc(on_ps, 1)

            def rwkv_prep(l):
                pe.wait_ge(p_th, l + 1)
                pe.wait_ge(rw_conv, (l + 1) * RW_T + 2)
                n = 0
                for j in range(HT):
                    for q in range(2):
                        for d in range(2):
                            pe.wait_ge(p_ev, l * 16 + n + 1)
                            hf = slice(64 * d, 64 * d + 64)
                            for sl, dst in halves(4 * d + 2 * q):
                                last = pe.matmul(dst, SMALL[hf, q * 512 + j * P:q * 512 + (j + 1) * P],
                                                 A[hf, 12 + q, sl], start=True, stop=True)
                            last.then_inc(p_mm, 1)
                            n += 1
                pe.wait_ge(p_ev, l * 16 + 16 + 4)
                for j in range(HT):
                    pe.wait_ge(p_sq, l * HT + j + 1)
                    for sl, dst in halves(2 * j):
                        last = pe.matmul(dst, blk, TM[:, j, sl], start=True, stop=True)
                    last.then_inc(p_ss, 1)

            def rwkv(l):
                hd = [slice(0, 64), slice(64, 128)]

                def flat(t):
                    return t.rearrange("p a c -> p (a c)")

                def group(b, g, lhs, rhs, done):
                    for k in range(4):
                        h = 4 * g + k
                        last = pe.matmul(ps[:, b + g, k * P:(k + 1) * P], lhs[:, h], rhs[:, h],
                                         start=True, stop=True)
                    if done is not None:
                        last.then_inc(done, 1)

                pe.wait_ge(p_kn, (l + 1) * HT)
                settle(pe, "pe")
                with pe.Fori(0, RN) as i:
                    u = l * RN + i
                    pe.wait_ge(r_bk, u + 1)
                    for d in range(2):
                        vh = hd[1 - d]
                        for j in range(HT):
                            pe.transpose(ps[:, 4 + d, j * P:(j + 1) * P], flat(R_BK[:, d, j]), ident)
                            last = pe.matmul(ps[vh, 6, j * P:(j + 1) * P], R_T1[:, d, j], ident,
                                             start=True, stop=True)
                    last.then_inc(r_tv, 1)
                    pe.wait_ge(r_kr, u + 1)
                    pe.wait_ge(r_ye, u + 1)
                    for d in range(2):
                        for j in range(HT):
                            for e in range(2):
                                last = pe.matmul(ps[:, 2 * d + e, j * P:(j + 1) * P],
                                                 flat(R_BK[hd[e], d, j]), flat(R_KR[hd[e], d, j]),
                                                 start=True, stop=True)
                    last.then_inc(r_am_ps, 1)
                    pe.wait_ge(r_tve, u + 1)
                    pe.wait_ge(r_am, u + 1)
                    for h in range(8):
                        pe.matmul(ps[:, 6, h * 64:(h + 1) * 64], R_AKK[:, h], R_VS[:, h],
                                  start=h == 0, stop=False, skip_group_check=True)
                    for d in range(2):
                        for j in range(HT):
                            last = pe.matmul(ps[hd[d], 6, j * P:(j + 1) * P], R_KR[:, d, j, 0], R_ST[:, d, j],
                                             start=False, stop=True, skip_group_check=True)
                    last.then_inc(r_r, 1)
                    for g in range(2):
                        for k in range(4):
                            h = 4 * g + k
                            last = pe.matmul(ps[:, g, k * P:(k + 1) * P], R_UI[:, h], ident,
                                             start=True, stop=True)
                        last.then_inc(r_t, 1)
                    for n in range(1, len(INV)):
                        for g in range(2):
                            if n == 1:
                                pe.wait_ge(r_w, u * 12 + (g + 1))
                            else:
                                pe.wait_ge(r_xye, u * 10 + (2 * (n - 2) + g + 1))
                            group(0, g, R_UI, R_X, r_t)
                        for g in range(2):
                            pe.wait_ge(r_w, u * 12 + (2 * n + g + 1))
                            if n < len(INV) - 1:
                                group(2, g, R_Y, R_W, None)
                            group(4, g, R_W, R_Y, r_xy)
                    pe.wait_ge(r_re, u + 1)
                    pe.wait_ge(r_xye, (u + 1) * 10)
                    for h in range(8):
                        last = pe.matmul(ps[:, 7, h * 64:(h + 1) * 64], R_Y[:, h], R_RS[:, h],
                                         start=True, stop=True)
                    last.then_inc(r_sa, 1)
                    for d in range(2):
                        for j in range(HT):
                            o = (d * HT + j) * 64
                            pe.matmul(ps[:, 3, o:o + 64], R_ST[:, d, j], R_KR[:, d, j, 1],
                                      start=d == 0 and j == 0, stop=False, skip_group_check=True)
                    pe.wait_ge(r_sae, u + 1)
                    for d in range(2):
                        for j in range(HT):
                            o = (d * HT + j) * 64
                            for e in range(2):
                                last = pe.matmul(ps[hd[e], 2, o:o + 64], R_BKT[:, d, j, e * 64:(e + 1) * 64],
                                                 R_SAV[:, d, 2 * j + e], start=True, stop=True)
                    last.then_inc(r_s, 1)
                    for d in range(2):
                        for j in range(HT):
                            o = (d * HT + j) * 64
                            for e in range(2):
                                last = pe.matmul(ps[hd[e], 3, o:o + 64], R_SAV[:, d, 2 * j + e],
                                                 R_AMR[:, d, 2 * j + e], start=False, stop=True,
                                                 skip_group_check=True)
                    last.then_inc(r_y, 1)

            def y_post(l):
                for j in range(HT):
                    u = l * HT + j
                    pe.wait_ge(q_a, u + 1)
                    for sl, dst in halves(0):
                        last = pe.matmul(dst, blk, YB[:, j, sl], start=True, stop=True)
                    last.then_inc(q_b, 1)
                    pe.wait_ge(q_c, u + 1)
                    for sl, dst in halves(2):
                        pe.matmul(dst, blk, TM[:, 1, sl], start=True, stop=True)
                    for sl, dst in halves(4):
                        pe.matmul(dst, blk, TM[:, 2, sl], start=True, stop=True)
                    for sl, dst in halves(6):
                        last = pe.matmul(dst, SMALL[:, 1024 + j * P:1024 + (j + 1) * P], A[:, 14, sl],
                                         start=True, stop=True)
                    last.then_inc(q_d, 1)

            pe.wait_ge(cst_in_sem, 32)
            pe.wait_ge(dve_setup, 1)
            settle(pe, "pe")
            with pe.Fori(0, DEPTH) as l:
                norm(l, norms[0])
                ffn(l, 0, S_UP1, S_DN1)
                norm(l, norms[1])
                pe.wait_ge(norms[1].h_ready, l + 1)
                settle(pe, "pe")
                project(l, S_HG, HG_T, HG_T // RING, H, hg_ev)
                gla(l)
                o_norm(l)
                pe.wait_ge(on_std, (l + 1) * HT)
                settle(pe, "pe")
                project(l, S_RW, RW_T, RW_T // RING, H, rw_ev)
                pe.wait_ge(par_loaded, 32 * (l + 1))
                rwkv_prep(l)
                rwkv(l)
                y_post(l)
                pe.wait_ge(q_f, (l + 1) * HT)
                pe.wait_ge(reloaded, 32 * (l + 1))
                settle(pe, "pe")
                project(l, S_OUT, KT, KT // RING, MX, out_res)
                norm(l, norms[2])
                ffn(l, 1, S_UP2, S_DN2)
            norm(0, fnorm)

        @block.scalar
        def _(act):
            activation = ordered(act, act.activation)

            def norm(l, s, ready, value):
                act.wait_ge(ready, value)
                for k in range(KT):
                    if k >= 2:
                        act.wait_ge(s.sq_used, l * KT + k - 1)
                    activation(TM[:, k % 2], X[:, k], ACT.Square).then_inc(s.sq_ready, 1)
                act.wait_ge(s.sq_used, l * KT + KT)
                for sl, src in halves(0):
                    activation(TM[:, 2, sl], src, ACT.Sqrt, bias=eps_rms, scale=1.0 / D).then_inc(s.std_ready, 1)

            def ffn(l, n, up):
                s = ffns[n]
                with act.Fori(0, FT // 2) as i:
                    for j in range(2):
                        act.wait_ge(w_used, l * SLOTS + i * 4 + (up + 2 * (j + 1)))
                        act.wait_ge(s.act_done, l * FT + i * 2 + (j + 1))
                        for sl, src in halves(4 * j):
                            last = activation(TM[:, j, sl], src, ACT.Silu)
                        last.then_inc(s.silu_done, 1)

            def gla(l):
                for t in (0, 1, 2, 3, 16, 17, 18, 19):
                    last = activation(A[:, t], A[:, t], ACT.Silu)
                last.then_inc(hg_silu, 1)
                act.wait_ge(spilled, 16 * (l + 1))
                settle(act, "act")
                with act.Fori(0, HT) as h:
                    u = l * HT + h
                    activation(G_QS, A[:, bass.ds(h, 1)].rearrange("p a t -> p (a t)"), ACT.Copy)
                    activation(G_IS, A[:, bass.ds(h + 12, 1)].rearrange("p a t -> p (a t)"),
                                   ACT.Copy).then_inc(g_in, 1)
                    act.wait_ge(g_vt_ps, u + 1)
                    activation(G_VT.rearrange("p (a t) -> p a t", a=2), ps[:, 4:6, 0:384],
                                   ACT.Copy).then_inc(g_vt, 1)
                    for d in range(2):
                        v = u * 2 + (d + 1)
                        z = A[:, bass.ds(h + (4 + 4 * d), 1)].rearrange("p a t -> p (a t)")
                        if d == 0:
                            act.wait_ge(g_lb, u + 1)
                        else:
                            act.wait_ge(g_att, u * 16 + 8)
                        ta, tb_, ra, rb_ = G_E[0], G_E[1], G_Z[0], G_Z[1]
                        lnlb = LBH[:, d:d + 1]
                        activation(ta, z, ACT.Abs)
                        activation(tb_, z, ACT.Abs, bias=lnlb, scale=-1.0)
                        activation(ra, z, ACT.Relu, scale=-1.0)
                        activation(rb_, z, ACT.Relu, bias=lnlb, scale=-1.0)
                        activation(ta, ta, ACT.Exp, scale=-1.0)
                        activation(tb_, tb_, ACT.Exp, scale=-1.0)
                        activation(ta, ta, ACT.Ln, bias=1.0)
                        activation(tb_, tb_, ACT.Ln, bias=1.0).then_inc(g_gate, 1)
                        act.wait_ge(g_w, v)
                        activation(G_KS, tb_, ACT.Exp, scale=-1.0).then_inc(g_kx, 1)
                        act.wait_ge(g_k, v)
                        activation(G_QE[d], G_B, ACT.Exp)
                        activation(G_KE, ta, ACT.Exp).then_inc(g_qe, 1)
                        act.wait_ge(g_kt_ps, v)
                        activation(G_KET.rearrange("p (a t) -> p a t", a=2), ps[:, 4:6, 0:384],
                                       ACT.Copy).then_inc(g_kt, 1)
                        for n in range(len(LEVELS)):
                            act.wait_ge(g_dx, (u * 2 + d) * 7 + (n + 1))
                            activation(G_E[n % 2], G_E[n % 2], ACT.Exp).then_inc(g_ex, 1)
                    act.wait_ge(g_o_ps, u + 1)
                    activation(MX[:, bass.ds(h, 1)].rearrange("p b (a t) -> p (b a) t", a=2),
                                   ps[:, 6:8, 0:384], ACT.Copy).then_inc(g_o, 1)
                for h in range(HT):
                    activation(TM[:, h], MX[:, h], ACT.Square).then_inc(on_sq, 1)
                for h in range(HT):
                    act.wait_ge(on_ps, l * HT + h + 1)
                    for sl, src in halves(2 * h):
                        last = activation(xt(h)[:, sl], src, ACT.Sqrt, bias=eps_rms, scale=1.0 / P)
                    last.then_inc(on_std, 1)

            def project_hg(l):
                with act.Fori(0, HG_T // RING) as i:
                    for j in range(RING):
                        act.wait_ge(w_used, l * SLOTS + i * RING + (S_HG + j + 1))
                        dst = A[:, bass.ds(i * RING + j, 1)].rearrange("p a t -> p (a t)")
                        for sl, src in halves(2 * j):
                            last = activation(dst[:, sl], src, ACT.Copy)
                        last.then_inc(hg_ev, 1)

            def project_rw(l):
                def group(i, k):
                    for j in range(k):
                        act.wait_ge(w_used, l * SLOTS + i * RING + (S_RW + j + 1))
                        act.wait_ge(rw_conv, l * RW_T + i * RING + (j + 1))
                        for sl, src in halves(2 * j):
                            last = activation(TM[:, j % 2, sl], src, ACT.Copy)
                        last.then_inc(rw_ev, 1)
                with act.Fori(0, RW_T // RING) as i:
                    group(i, RING)
                group(RW_T // RING, RW_T % RING)

            def rwkv_prep(l):
                act.wait_ge(rw_conv, (l + 1) * RW_T + 2)
                activation(A[:, 12], A[:, 12], ACT.Tanh)
                activation(A[:, 14], A[:, 14], ACT.Sigmoid).then_inc(p_th, 1)
                n = 0
                for j in range(HT):
                    for q in range(2):
                        for d in range(2):
                            act.wait_ge(p_mm, l * 16 + n + 1)
                            dst = (R_lw, R_a)[q][d][:, j]
                            bias = par(("w0", "a0")[q], d * HT + j)
                            for sl, src in halves(4 * d + 2 * q):
                                last = activation(dst[:, sl], src, ACT.Sigmoid, bias=bias)
                            last.then_inc(p_ev, 1)
                            n += 1
                for j in range(HT):
                    act.wait_ge(p_kk, l * HT + j + 1)
                    activation(TM[:, j], R_kk[:, j], ACT.Square).then_inc(p_sq, 1)
                for j in range(HT):
                    act.wait_ge(p_mx, l * HT + j + 1)
                    activation(TM[:, j], TM[:, j], ACT.Sqrt).then_inc(p_sd, 1)

            def rwkv(l):
                def heads(t):
                    return t.rearrange("p (h c) -> p h c", h=8)

                def exponentials(u):
                    act.wait_ge(r_cum, u + 1)
                    for d in range(2):
                        activation(R_EP[:, d, :, 1 - d:1 - d + RC], R_T1[:, d], ACT.Exp)
                        last = activation(R_EI[:, d], R_T1[:, d], ACT.Exp, scale=-1.0)
                    last.then_inc(r_exp, 1)

                def step(u, more):
                    act.wait_ge(r_tv, u + 1)
                    v_ps = heads(ps[:, 6, :])
                    activation(R_VS, v_ps, ACT.Copy)
                    activation(R_BKT, ps[:, 4:6, :].rearrange("p d (j c) -> p d j c", j=HT), ACT.Copy)
                    activation(R_SAV[64:128, 0], v_ps[64:128], ACT.Copy)
                    activation(R_SAV[0:64, 1], v_ps[0:64], ACT.Copy).then_inc(r_tve, 1)
                    act.wait_ge(r_r, u + 1)
                    activation(R_RS, heads(ps[:, 6, :]), ACT.Copy, scale=-1.0).then_inc(r_re, 1)
                    for n in range(1, len(INV)):
                        for g in range(2):
                            act.wait_ge(r_xy, u * 10 + (2 * (n - 1) + g + 1))
                            q = slice(4 * g, 4 * g + 4)
                            if n < len(INV) - 1:
                                activation(R_X[:, q], ps[:, 2 + g, :].rearrange("p (h c) -> p h c", h=4), ACT.Copy)
                            activation(R_Y[:, q], ps[:, 4 + g, :].rearrange("p (h c) -> p h c", h=4),
                                       ACT.Copy).then_inc(r_xye, 1)
                        if n == 1 and more:
                            exponentials(u + 1)
                    act.wait_ge(r_sa, u + 1)
                    sa_ps = heads(ps[:, 7, :])
                    activation(R_SAV[0:64, 0], sa_ps[0:64], ACT.Copy)
                    activation(R_SAV[64:128, 1], sa_ps[64:128], ACT.Copy).then_inc(r_sae, 1)

                act.wait_ge(r_cum, l * RN + 1)
                settle(act, "act")
                exponentials(l * RN)
                with act.Fori(0, RN - 1) as i:
                    step(l * RN + i, True)
                step(l * RN + (RN - 1), False)

            def y_post(l):
                for j in range(HT):
                    u = l * HT + j
                    act.wait_ge(q_e, u + 1)
                    activation(TM[:, 1], YB[:, j], ACT.Square).then_inc(q_c, 1)
                    act.wait_ge(q_d, u + 1)
                    for sl, src in halves(2):
                        last = activation(TM[:, 3, sl], src, ACT.Sqrt, bias=eps_gn, scale=1.0 / 64)
                    last.then_inc(q_std, 1)

            act.wait_ge(cst_in_sem, 32)
            act.wait_ge(dve_setup, 2)
            activation(LG[:, 32:48], LG[:, 16:32], ACT.Exp).then_inc(act_setup, 1)
            act.wait_ge(dve_setup, 3)
            activation(LG[:, 56:64], LG[:, 48:56], ACT.Ln).then_inc(act_setup, 1)
            with act.Fori(0, DEPTH) as l:
                act.wait_ge(cvec_loaded, 16 * (l + 1))
                activation(CBC, CBC, ACT.Silu).then_inc(cvec_ready, 1)
                act.wait_ge(x_loaded, 16)
                norm(l, norms[0], mod_done, l + 1)
                ffn(l, 0, S_UP1)
                norm(l, norms[1], ffns[0].res_done, (l + 1) * KT + 4)
                project_hg(l)
                gla(l)
                act.wait_ge(on_done, l + 1)
                project_rw(l)
                rwkv_prep(l)
                rwkv(l)
                y_post(l)
                norm(l, norms[2], out_res, (l + 1) * KT + 4)
                ffn(l, 1, S_UP2)
                act.nop().then_inc(layer_done_act, 1)
            norm(0, fnorm, ffns[1].res_done, DEPTH * KT + 4)

        @block.vector
        def _(dve):
            tt, ts, stt = (ordered(dve, f) for f in (dve.tensor_tensor, dve.tensor_scalar, dve.scalar_tensor_tensor))
            tensor_copy, memset, reciprocal, copy_predicated, tensor_tensor_scan, tensor_tensor_reduce = (
                ordered(dve, f) for f in (dve.tensor_copy, dve.memset, dve.reciprocal, dve.copy_predicated,
                                          dve.tensor_tensor_scan, dve.tensor_tensor_reduce))

            def norm(l, s, n):
                dve.wait_ge(s.std_ready, 2 * (l + 1))
                reciprocal(TM[:, 3], TM[:, 2])
                for k in range(KT):
                    tt(H[:, k], X[:, k], TM[:, 3], ALU.mult)
                for k in range(KT):
                    if n is None:
                        last = ts(H[:, k], H[:, k], CST[:, C_FG + k:C_FG + k + 1], None, ALU.mult)
                    else:
                        for q, sl in ((1, slice(0, CTX)), (0, slice(CTX, T))):
                            last = ts(H[:, k, sl], H[:, k, sl], coef[:, n, 0, k, q:q + 1],
                                      coef[:, n, 1, k, q:q + 1], ALU.mult, ALU.add)
                last.then_inc(s.h_ready, 1)

            def residual(l, n, first, slots, done):
                with dve.Fori(0, 2) as g:
                    for m in range(4):
                        dve.wait_ge(w_used, l * SLOTS + g * (4 * slots) + (first + slots * (m + 1)))
                        xk = X[:, bass.ds(g * 4 + m, 1)].rearrange("p a t -> p (a t)")
                        ck = coef[:, n, 2, bass.ds(g * 4 + m, 1)].rearrange("p a s -> p (a s)")
                        for q, (sl, src) in zip((1, 0), halves(2 * m)):
                            last = stt(xk[:, sl], src, ck[:, q:q + 1], xk[:, sl], ALU.mult, ALU.add)
                        last.then_inc(done, 1)

            def ffn(l, n):
                s = ffns[n]
                with dve.Fori(0, FT // 2) as i:
                    for j in range(2):
                        dve.wait_ge(s.silu_done, l * FT + i * 2 + (j + 1))
                        dst = A[:, bass.ds(i * 2 + j, 1)].rearrange("p a t -> p (a t)")
                        for sl, src in halves(4 * j + 2):
                            last = tt(dst[:, sl], TM[:, j, sl], src, ALU.mult)
                        last.then_inc(s.act_done, 1)
                residual(l, 2 * n, (S_DN1, S_DN2)[n], 3, s.res_done)

            def modulation(l):
                dve.wait_ge(cvec_ready, l + 1)
                dve.wait_ge(par_loaded, 32 * (l + 1))
                settle(dve, "dve")
                bm = PAR[:, COLS["b_mod"][0]:COLS["b_mod"][1]]
                with dve.Fori(0, MT // RING) as i:
                    for j in range(RING):
                        dve.wait_ge(w_ready[j], slot_value(l, S_MOD, i))
                        for q in range(2):
                            last = tensor_tensor_reduce(JUNK[:, q], W[j], CBC[:, q], 1.0, 0.0, ALU.mult, ALU.add,
                                                            MTMP[:, 2 * j + q:2 * j + q + 1])
                        last.then_inc(w_used, 1)
                    tt(MOD[:, bass.ds(i * 2 * RING, 2 * RING)].rearrange("p (k s) -> p k s", s=2),
                       MTMP[:, :].rearrange("p (k s) -> p k s", s=2),
                       bm[:, bass.ds(i * RING, RING)].unsqueeze(2).to_broadcast([P, RING, 2]), ALU.add)
                for n in range(3):
                    g = par("gain", n * KT, KT).unsqueeze(2).to_broadcast([P, KT, 2])
                    stt(coef[:, n, 0], modv[:, 3 * n + 1], 1.0, g, ALU.add, ALU.mult)
                    tensor_copy(coef[:, n, 1], modv[:, 3 * n])
                    ts(coef[:, n, 2], modv[:, 3 * n + 2], 1.0 if n == 1 else 0.5, None, ALU.mult)
                ts(KAX[:, 0:HT], par("k_a", 0, HT), -1.0, 1.0, ALU.mult, ALU.add)
                ts(KAX[:, HT:], par("k_a", 0, HT), -2.0, 2.0, ALU.mult, ALU.add)
                dve.nop().then_inc(mod_done, 1)

            def chunked(t):
                return t.rearrange("p (c t) -> p c t", t=GC)

            def gla(l):
                dve.wait_ge(hg_silu, l + 1)
                dve.wait_ge(spilled, 16 * (l + 1))
                settle(dve, "dve")
                with dve.Fori(0, HT) as h:
                    u = l * HT + h
                    lbl = LBC[:, bass.ds(l * 16 + h, 13)]
                    tensor_copy(LBH[:, :], lbl[:, 0:13:4]).then_inc(g_lb, 1)
                    for d in range(2):
                        v = u * 2 + (d + 1)
                        n7, n8 = (u * 2 + d) * 7, (u * 2 + d) * 8
                        z = A[:, bass.ds(h + (4 + 4 * d), 1)].rearrange("p a t -> p (a t)")
                        ta, tb_, ra, rb_ = G_E[0], G_E[1], G_Z[0], G_Z[1]
                        dve.wait_ge(g_gate, v)
                        tt(ta, ta, ra, ALU.add)
                        tt(rb_, rb_, tb_, ALU.add)
                        tt(tb_, ta, z, ALU.add).then_inc(g_w, 1)
                        tt(rb_, rb_, ta, ALU.subtract)
                        for c in range(GN):
                            sl = slice(c * GC, (c + 1) * GC)
                            o, src = G_B[:, sl], rb_[:, sl]
                            if d == 1:
                                o, src = o[:, ::-1], src[:, ::-1]
                            tensor_tensor_scan(o, ones, src, 0.0, ALU.mult, ALU.add)
                        last_t = 0 if d else GC - 1
                        b3 = chunked(G_B)
                        tt(chunked(ta), b3[:, :, last_t:last_t + 1].to_broadcast([P, GN, GC]), b3, ALU.subtract)
                        dve.wait_ge(g_kx, v)
                        ts(G_KS, G_KS, LBH[:, 2 + d:3 + d], None, ALU.mult)
                        dve.nop().then_inc(g_k, 1)
                        dve.wait_ge(g_qe, v)
                        tensor_copy(EBL[:, :].unsqueeze(2), chunked(G_QE[d])[:, :, last_t:last_t + 1])
                        tt(G_KE, G_KE, G_KS, ALU.mult)
                        tt(G_QE[d], G_QE[d], G_QS, ALU.mult).then_inc(g_ke, 1)

                        def sides(t, m):
                            w = t.rearrange("p (b s m) -> p b s m", s=2, m=m)
                            return w[:, :, 1 - d], w[:, :, d]

                        def exponents(n):
                            m = LEVELS[n]
                            bq, bk = sides(G_B, m)
                            eq, ek = sides(G_E[n % 2], m)
                            at_ = 0 if d else m - 1
                            ref = bk[:, :, at_:at_ + 1].to_broadcast([P, T // (2 * m), m])
                            tt(eq, bq, ref, ALU.subtract)
                            tt(ek, ref, bk, ALU.subtract).then_inc(g_dx, 1)

                        def scale(n):
                            m = LEVELS[n]
                            dve.wait_ge(g_ex, n7 + (n + 1))
                            if n >= 2:
                                dve.wait_ge(g_att_ps, n8 + n)
                            eq, ek = sides(G_E[n % 2], m)
                            zq, zk = sides(G_Z[n % 2], m)
                            tt(zq, eq, sides(G_QS, m)[0], ALU.mult)
                            tt(zk, ek, sides(G_KS, m)[1], ALU.mult).then_inc(g_z, 1)

                        def merge(n):
                            dve.wait_ge(g_att_ps, n8 + (n + 2))
                            settle(dve, "dve")
                            b = 2 * ((n + 1) % 2)
                            o = C_LVL + (d * len(LEVELS) + n) * P
                            for a in range(2):
                                mask = CST[:, o:o + P].bitcast(U32).unsqueeze(1).to_broadcast([P, 3, GC])
                                copy_predicated(chunked(G_ATT[d])[:, 3 * a:3 * a + 3], mask,
                                                    ps[:, b + a, 0:384].rearrange("p (c t) -> p c t", t=GC))
                            dve.nop().then_inc(g_att, 1)

                        exponents(0)
                        dve.wait_ge(g_att_ps, n8 + 1)
                        for a in range(2):
                            tt(chunked(G_ATT[d])[:, 3 * a:3 * a + 3],
                               ps[:, a, 0:384].rearrange("p (c t) -> p c t", t=GC),
                               ident.unsqueeze(1).to_broadcast([P, 3, GC]), ALU.mult)
                        dve.nop().then_inc(g_att, 1)
                        for n in range(len(LEVELS)):
                            if n + 1 < len(LEVELS):
                                exponents(n + 1)
                            scale(n)
                            if n >= 1:
                                merge(n - 1)
                            if n == 2:
                                dve.wait_ge(g_u, v)
                                order = GLA_ORDER[d]
                                for a, c in enumerate(order[:-1]):
                                    nxt = order[a + 1]
                                    dst = G_S[d][:, nxt * GC:(nxt + 1) * GC]
                                    src = ps[:, 4 + c // 3, (c % 3) * GC:(c % 3 + 1) * GC]
                                    if a == 0:
                                        last = tensor_copy(dst, src)
                                    else:
                                        last = stt(dst, G_S[d][:, c * GC:(c + 1) * GC], EBL[:, c:c + 1], src,
                                                   ALU.mult, ALU.add)
                                dve.nop().then_inc(g_s, 1)
                        merge(len(LEVELS) - 1)
                for h in range(HT):
                    dve.wait_ge(on_std, l * HT + h + 1)
                    reciprocal(xt(h), xt(h))
                    stt(MX[:, h], MX[:, h], par("ogain", h), xt(h), ALU.mult, ALU.mult)
                    last = tt(MX[:, h], MX[:, h], A[:, 16 + h], ALU.mult)
                last.then_inc(on_done, 1)

            def convolve(l):
                def group(i, k):
                    for j in range(k):
                        dve.wait_ge(rw_ev, l * RW_T + i * RING + (j + 1) + 4)
                        src = TM[:, j % 2]
                        dst = A[:, bass.ds(i * RING + j, 1)].rearrange("p a t -> p (a t)")
                        a0 = COLS["taps"][0]
                        taps = PAR[:, a0:a0 + RW_T * 9][:, bass.ds((i * RING + j) * 9, 9)]
                        ts(dst, src, taps[:, 4:5], None, ALU.mult)
                        stt(dst[:, 1:CTX], src[:, 0:CTX - 1], taps[:, 3:4], dst[:, 1:CTX], ALU.mult, ALU.add)
                        stt(dst[:, 0:CTX - 1], src[:, 1:CTX], taps[:, 5:6], dst[:, 0:CTX - 1], ALU.mult, ALU.add)
                        sg = src[:, CTX:T].rearrange("p (y x) -> p y x", x=GRID_W)
                        dg = dst[:, CTX:T].rearrange("p (y x) -> p y x", x=GRID_W)
                        for dy in (-1, 0, 1):
                            for dx in (-1, 0, 1):
                                if dy == 0 and dx == 0:
                                    continue
                                y0, y1 = max(0, -dy), GRID_H - max(0, dy)
                                x0, x1 = max(0, -dx), GRID_W - max(0, dx)
                                n = (dy + 1) * 3 + dx + 1
                                o = dg[:, y0:y1, x0:x1]
                                last = stt(o, sg[:, y0 + dy:y1 + dy, x0 + dx:x1 + dx], taps[:, n:n + 1], o,
                                           ALU.mult, ALU.add)
                        last.then_inc(rw_conv, 1)
                with dve.Fori(0, RW_T // RING) as i:
                    group(i, RING)
                group(RW_T // RING, RW_T % RING)

            def rwkv_prep(l):
                for j in range(HT):
                    ts(R_kk[:, j], R_k[:, j], par("k_k", j), None, ALU.mult).then_inc(p_kk, 1)
                dve.wait_ge(p_ev, l * 16 + 16 + 4)
                for d in range(2):
                    ts(R_lw[d], R_lw[d], -RSQRT_E, None, ALU.mult)
                for j in range(HT):
                    dve.wait_ge(p_ss, l * HT + j + 1)
                    for sl, src in halves(2 * j):
                        last = ts(TM[:, j, sl], src, 1e-24, None, ALU.max)
                    last.then_inc(p_mx, 1)
                for j in range(HT):
                    dve.wait_ge(p_sd, l * HT + j + 1)
                    reciprocal(TM[:, j], TM[:, j])
                    tt(R_kk[:, j], R_kk[:, j], TM[:, j], ALU.mult).then_inc(p_kn, 1)

            def rwkv(l):
                hd = [slice(0, 64), slice(64, 128)]
                dve.wait_ge(o_spilled, 16 * (l + 1))
                settle(dve, "dve")
                for z in (R_STF, YB, R_AKK, R_UI):
                    memset(z, 0.0)
                for d in range(2):
                    tensor_copy(R_UI[hd[d], :, hd[d]], ident[hd[d], hd[d]].unsqueeze(1).to_broadcast([64, 8, 64]))
                memset(R_EP[:, 0, :, 0:1], 1.0)
                memset(R_EP[:, 1, :, RC:RC + 1], 1.0)
                ka = par("k_a", 0, HT).unsqueeze(2).to_broadcast([P, HT, RC])
                oka = KAX[:, 0:HT].unsqueeze(2).to_broadcast([P, HT, RC])
                bs, ks = (0, 1), (1, 0)

                def chunk(t, c):
                    return t[:, :, bass.ds(c * RC, RC)]

                def cumulate(c):
                    tensor_copy(R_EI[:, 1], chunk(R_lw[1], c[1]))
                    for j in range(HT):
                        tensor_tensor_scan(R_T1[:, 0, j], ones[:, 0:RC], chunk(R_lw[0], c[0])[:, j], 0.0,
                                           ALU.mult, ALU.add)
                        last = tensor_tensor_scan(R_T1[:, 1, j, ::-1], ones[:, 0:RC], R_EI[:, 1, j, ::-1], 0.0,
                                                  ALU.mult, ALU.add)
                    last.then_inc(r_cum, 1)

                def scale_bk(c, d, part):
                    if part == 0:
                        tt(R_BK[:, d, :, bs[d]], chunk(R_kk, c[d]), chunk(R_a[d], c[d]), ALU.mult)
                        tt(R_BK[:, d, :, ks[d]], chunk(R_a[d], c[d]), ka, ALU.mult)
                        tt(R_BK[:, d, :, bs[d]], R_BK[:, d, :, bs[d]], R_EI[:, d], ALU.mult)
                        tensor_copy(R_T1[:, d], chunk(R_v, c[d]))
                    else:
                        tt(R_BK[:, d, :, ks[d]], R_BK[:, d, :, ks[d]], oka, ALU.add)
                        tt(R_BK[:, d, :, ks[d]], R_BK[:, d, :, ks[d]], chunk(R_k, c[d]), ALU.mult)
                        last = tt(R_BK[:, d, :, ks[d]], R_BK[:, d, :, ks[d]], R_EI[:, d], ALU.mult)
                        if d == 1:
                            last.then_inc(r_bk, 1)

                def scale_kr(c):
                    for d in range(2):
                        prev, here, end = (0, 1, RC) if d == 0 else (1, 0, 0)
                        tensor_copy(PCT[:, d * HT:(d + 1) * HT].unsqueeze(2), R_EP[:, d, :, end:end + 1])
                        tt(R_KR[:, d, :, 0], chunk(R_kk, c[d]), R_EP[:, d, :, prev:prev + RC], ALU.mult)
                        last = tt(R_KR[:, d, :, 1], chunk(R_r, c[d]), R_EP[:, d, :, here:here + RC], ALU.mult)
                    last.then_inc(r_kr, 1)

                def step(u, c, nxt):
                    dve.wait_ge(r_am_ps, u + 1)
                    settle(dve, "dve")
                    strict = [CST[:, C_AM + d * P:C_AM + d * P + 64] for d in range(2)]
                    for d in range(2):
                        am = ps[:, 2 * d:2 * d + 2, :].rearrange("p e (j c) -> p e j c", j=HT)
                        for e in range(2):
                            copy_predicated(R_UI[hd[d], e:8:2, hd[d]],
                                            strict[d][hd[d]].bitcast(U32).unsqueeze(1).to_broadcast([64, HT, 64]),
                                            am[hd[d], e, :, 0:64])
                            q = hd[1 - d]
                            tt(R_AKK[q, e:8:2, hd[d]], am[q, e, :, 0:64],
                               strict[d][q].unsqueeze(1).to_broadcast([64, HT, 64]), ALU.mult)
                    for d in range(2):
                        am = ps[:, 2 * d:2 * d + 2, :].rearrange("p e (j c) -> p e j c", j=HT)
                        incl = CST[:, C_AM + d * P + 64:C_AM + (d + 1) * P].unsqueeze(1).to_broadcast([P, HT, 64])
                        for e in range(2):
                            last = tt(R_AMR[:, d, e:8:2], am[:, e, :, 64:128], incl, ALU.mult)
                    last.then_inc(r_am, 1)
                    for n in range(len(INV)):
                        o = C_INV + n * P
                        m = CST[:, o:o + P].unsqueeze(1).to_broadcast([P, 4, P])
                        for g in range(2):
                            q = slice(4 * g, 4 * g + 4)
                            if n == 0:
                                tt(R_Y[:, q], R_UI[:, q],
                                   CST[:, C_INV0T:C_INV0T + P].unsqueeze(1).to_broadcast([P, 4, P]), ALU.mult)
                            dve.wait_ge(r_t, u * 12 + (2 * n + g + 1))
                            tt((R_X if n == 0 else R_W)[:, q], ps[:, g, :].rearrange("p (h c) -> p h c", h=4), m,
                               ALU.mult).then_inc(r_w, 1)
                        if nxt is not None:
                            if n == 0:
                                cumulate(nxt)
                            if n == 2:
                                dve.wait_ge(r_exp, u + 2)
                            if n >= 2:
                                scale_bk(nxt, (n - 2) // 2, (n - 2) % 2)
                    dve.wait_ge(r_s, u + 1)
                    for e in range(2):
                        q = hd[e]
                        s = R_STF[q].rearrange("p (g c) -> p g c", c=P)[:, :, hd[e]]
                        tt(s, s, ps[q, 2, :].rearrange("p (g c) -> p g c", c=64), ALU.add)
                        tt(s, s, PCT[q].unsqueeze(2).to_broadcast([64, 2 * HT, 64]), ALU.mult)
                    dve.wait_ge(r_y, u + 1)
                    if nxt is not None:
                        scale_kr(nxt)
                    for d in range(2):
                        y = chunk(YB, c[d])
                        last = tt(y, y, ps[:, 3, d * 256:(d + 1) * 256].rearrange("p (j c) -> p j c", j=HT), ALU.add)
                    last.then_inc(r_ye, 1)

                def pair(i, mirror):
                    return (i, mirror - i)

                u0 = l * RN
                m_ctx, m_lat = RN_CTX - 1, RN + RN_CTX - 1
                first = pair(0, m_ctx)
                cumulate(first)
                dve.wait_ge(r_exp, u0 + 1)
                for d in range(2):
                    for part in range(2):
                        scale_bk(first, d, part)
                scale_kr(first)
                with dve.Fori(0, RN_CTX - 1) as i:
                    step(u0 + i, pair(i, m_ctx), pair(i + 1, m_ctx))
                step(u0 + (RN_CTX - 1), pair(RN_CTX - 1, m_ctx), pair(RN_CTX, m_lat))
                with dve.Fori(RN_CTX, RN - 1) as i:
                    step(u0 + i, pair(i, m_lat), pair(i + 1, m_lat))
                step(u0 + (RN - 1), pair(RN - 1, m_lat), None)

            def y_post(l):
                for j in range(HT):
                    u = l * HT + j
                    tt(TM[:, 2], R_a[0][:, j], R_a[1][:, j], ALU.add)
                    ts(TM[:, 2], TM[:, 2], par("k_a", j), KAX[:, HT + j:HT + j + 1], ALU.mult, ALU.add)
                    tt(TM[:, 2], TM[:, 2], R_k[:, j], ALU.mult)
                    tt(TM[:, 2], TM[:, 2], R_r[:, j], ALU.mult)
                    ts(TM[:, 2], TM[:, 2], par("r_k", j), None, ALU.mult)
                    dve.nop().then_inc(q_a, 1)
                    dve.wait_ge(q_b, u + 1)
                    for sl, src in halves(0):
                        stt(YB[:, j, sl], src, -1.0 / 64, YB[:, j, sl], ALU.mult, ALU.add)
                    dve.nop().then_inc(q_e, 1)
                    dve.wait_ge(q_std, u + 1)
                    reciprocal(TM[:, 3], TM[:, 3])
                    tt(YB[:, j], YB[:, j], TM[:, 3], ALU.mult)
                    for sl, src in halves(4):
                        tt(TM[:, 2, sl], R_v[:, j, sl], src, ALU.mult)
                    ts(YB[:, j], YB[:, j], par("ln_w", j), par("ln_b", j), ALU.mult, ALU.add)
                    tt(YB[:, j], YB[:, j], TM[:, 2], ALU.add)
                    for sl, src in halves(6):
                        last = tt(YB[:, j, sl], YB[:, j, sl], src, ALU.mult)
                    last.then_inc(q_f, 1)

            dve.wait_ge(cst_in_sem, 32)
            for s, n in ([(f.act_done, 2) for f in ffns] + [(f.res_done, 4) for f in ffns] +
                         [(layer_done_dve, 1), (layer_done_act, 1), (hg_ev, 4), (rw_ev, 4), (rw_conv, 2), (out_res, 4), (p_ev, 4), (r_ye, 1)]):
                dve.nop().then_inc(s, n)
            memset(EPS[:, 0:1], RMS_EPS)
            memset(EPS[:, 1:2], GN_EPS)
            dve.nop().then_inc(dve_setup, 1)
            tt(LG[:, 48:56], LG[:, 0:8], LG[:, 8:16], ALU.max)
            tt(LG[:, 16:24], LG[:, 0:8], LG[:, 48:56], ALU.subtract)
            tt(LG[:, 24:32], LG[:, 8:16], LG[:, 48:56], ALU.subtract).then_inc(dve_setup, 1)
            dve.wait_ge(act_setup, 1)
            tt(LG[:, 48:56], LG[:, 32:40], LG[:, 40:48], ALU.add).then_inc(dve_setup, 1)
            dve.wait_ge(act_setup, 2)
            memset(LBC[:, 0:8], NEVER)
            memset(LBC[:, 8:16], 1.0)
            tt(LBC[:, 16:24], LG[:, 24:32], LG[:, 56:64], ALU.subtract)
            reciprocal(LG[:, 48:56], LG[:, 48:56])
            tt(LBC[:, 24:32], LG[:, 32:40], LG[:, 48:56], ALU.mult)

            with dve.Fori(0, DEPTH) as l:
                modulation(l)
                norm(l, norms[0], 0)
                ffn(l, 0)
                norm(l, norms[1], 1)
                gla(l)
                convolve(l)
                rwkv_prep(l)
                rwkv(l)
                y_post(l)
                dve.nop().then_inc(xr_free, 1)
                dve.wait_ge(reloaded, 32 * (l + 1))
                settle(dve, "dve")
                residual(l, 1, S_OUT, 1, out_res)
                norm(l, norms[2], 2)
                ffn(l, 1)
                dve.nop().then_inc(layer_done_dve, 1)
            norm(0, fnorm, None)


def constants(np):
    c = np.zeros((P, NCST), np.float32)
    c[:, C_ID:C_ID + P] = np.eye(P)
    c[:, C_ONE:C_ONE + P] = 1.0
    c[:64, C_BLK:C_BLK + 64] = 1.0
    c[64:, C_BLK + 64:C_BLK + P] = 1.0
    s, t = np.arange(GC)[:, None], np.arange(GC)[None, :]
    for n, m in enumerate(LEVELS):
        fw = (s // (2 * m) == t // (2 * m)) & (s // m % 2 == 0) & (t // m % 2 == 1)
        c[:, C_LVL + n * P:C_LVL + (n + 1) * P] = fw
        c[:, C_LVL + (len(LEVELS) + n) * P:C_LVL + (len(LEVELS) + n + 1) * P] = fw.T
    i, t = np.arange(RC)[:, None], np.arange(RC)[None, :]
    fw = np.concatenate([i < t, i <= t], axis=1)
    bw = np.concatenate([i > t, i >= t], axis=1)
    c[:, C_AM:C_AM + P] = np.concatenate([fw, fw])
    c[:, C_AM + P:C_AM + 2 * P] = np.concatenate([bw, bw])
    for n, m in enumerate(INV):
        fw = (i // (2 * m) == t // (2 * m)) & (i // m % 2 == 0) & (t // m % 2 == 1)
        lvl = np.eye(P, dtype=np.float32)
        lvl[:64, :64] -= fw.T
        lvl[64:, 64:] -= fw
        c[:, C_INV + n * P:C_INV + (n + 1) * P] = lvl
        if n == 0:
            c[:, C_INV0T:C_INV0T + P] = lvl.T
    return c


def kernel(**inputs):
    import numpy as np
    import concourse.bacc as bacc
    from concourse.bass_utils import run_bass_kernel_spmd

    v = {k: np.asarray(a) for k, a in inputs.items()}

    def by_tile(a):
        return np.moveaxis(a.reshape(-1, P), 0, 1)

    def columns(w):
        k, m = w.shape
        return w.reshape(k // P, P, m // P, P).transpose(2, 1, 0, 3).reshape(m // P, P, -1)

    stream = np.zeros((DEPTH * SLOTS, P, 1024), np.float32)
    par_a = np.zeros((DEPTH, P, NPAR), np.float32)
    small = np.zeros((DEPTH, P, 3 * 512), np.float32)
    for l in range(DEPTH):
        s = stream[l * SLOTS:(l + 1) * SLOTS]
        s[S_MOD:S_UP1] = v["w_mod"][l].T.reshape(MT, P, D)
        for n, (up, dn) in enumerate(((S_UP1, S_DN1), (S_UP2, S_DN2))):
            w = columns(v[f"ffn{n + 1}_up"][l])
            s[up:up + 2 * FT:2] = w[:FT]
            s[up + 1:up + 2 * FT:2] = w[FT:]
            w = columns(v[f"ffn{n + 1}_down"][l])
            k0 = 0
            for r, nk in enumerate(DOWN_K):
                s[dn + r:dn + 3 * KT:3, :, 0:nk * P] = w[:, :, k0 * P:(k0 + nk) * P]
                k0 += nk
        w = columns(v["w_in"][l])
        s[S_HG:S_HG + HG_T] = w[:HG_T]
        s[S_RW:S_RW + RW_T] = w[HG_T:]
        s[S_OUT:S_OUT + KT] = columns(v["w_out"][l])
        for name, a in (("gain", by_tile(v["norm_gains"][l])), ("ogain", by_tile(v["hgrn_o_gain"][l])),
                        ("taps", v["rwkv_conv"][l].reshape(9, RW_T, P).transpose(2, 1, 0).reshape(P, -1)),
                        ("w0", by_tile(v["rwkv_w0"][l])), ("a0", by_tile(v["rwkv_a0"][l])),
                        ("k_k", by_tile(v["rwkv_k_k"][l])), ("k_a", by_tile(v["rwkv_k_a"][l])),
                        ("r_k", by_tile(v["rwkv_r_k"][l])), ("ln_w", by_tile(v["rwkv_ln_w"][l])),
                        ("ln_b", by_tile(v["rwkv_ln_b"][l])), ("b_mod", by_tile(v["b_mod"][l]))):
            a0, a1 = COLS[name]
            par_a[l, :, a0:a1] = a
        small[l, :, 0:512] = v["rwkv_w_up"][l].reshape(P, 512)
        small[l, :, 512:1024] = v["rwkv_a_up"][l].reshape(P, 512)
        small[l, :, 1024:] = v["rwkv_g_up"][l]
    cst = constants(np)
    cst[:, C_FG:C_FG + KT] = by_tile(v["final_gain"])
    tokens = np.concatenate([v["ctx"][0], v["x"][0]])
    x_in = np.ascontiguousarray(tokens.T.reshape(KT, P, T).transpose(1, 0, 2))
    cvec = np.ascontiguousarray(np.broadcast_to(np.concatenate([v["c"][0], v["c_ctx"]])[None], (P, 2 * D)))
    arrays = {"x_in": x_in, "wstream": stream, "par_in": par_a, "small_in": small, "cst_in": cst,
              "logit_in": np.ascontiguousarray(by_tile(v["hgrn_lb_logits"])), "cvec_in": cvec}

    nc = bacc.Bacc("TRN2", target_bir_lowering=False, num_devices=1)
    args = [nc.dram_tensor(n, a.shape, F32, kind="ExternalInput").ap() for n, a in arrays.items()]
    out = nc.dram_tensor("out", (P, KT, LAT), F32, kind="ExternalOutput").ap()
    build_program(nc, *args, out)
    r = run_bass_kernel_spmd(nc, [arrays], core_ids=[0])
    got = r.results[0]["out"]
    return np.ascontiguousarray(got.transpose(2, 1, 0).reshape(1, LAT, D))
```

```python
from contextlib import ExitStack

import concourse.bass as bass
from concourse import mybir

F32 = mybir.dt.float32
U32 = mybir.dt.uint32
F32R = mybir.dt.float32r
ALU = mybir.AluOpType
ACT = mybir.ActivationFunctionType

P = 128
DEPTH = 2
D = 1024
KT = D // P
CTX, LAT = 256, 512
T = CTX + LAT
GRID_W = 64
GRID_H = LAT // GRID_W
F = 2816
FT = F // P
HT = 4
N_MOD = 9
MT = N_MOD * KT
HG_T = 5 * HT
RW_T = 15
RMS_EPS, GN_EPS = 1e-6, 64e-5
RSQRT_E = 0.6065306597126334
NEVER = -1e30

RING = 4
S_UP1 = 0
S_DN1 = S_UP1 + 2 * FT
S_HG = S_DN1 + 3 * KT
S_RW = S_HG + HG_T
S_OUT = S_RW + RW_T + 1
S_UP2 = S_OUT + KT
S_DN2 = S_UP2 + 2 * FT
SLOTS = S_DN2 + 3 * KT
assert all(s % RING == 0 for s in (S_UP1, S_DN1, S_HG, S_RW, S_OUT, S_UP2, S_DN2, SLOTS))
DOWN_K = (8, 8, FT - 16)

MG = MT // RING
MG_NEXT = 2 * KT // RING
MG_GATE = 3 * KT // RING
MG_FFN = 5 * KT // RING

UPS = 2 * FT
HALF = KT // 2

COLS = {}
_n = 0
for _name, _w in (("gain", 3 * KT), ("ogain", HT), ("taps", RW_T * 9), ("w0", 2 * HT), ("a0", 2 * HT),
                  ("k_k", HT), ("k_a", HT), ("r_k", HT), ("ln_w", HT), ("ln_b", HT), ("b_mod", MT)):
    COLS[_name] = (_n, _n + _w)
    _n += _w
NPAR = _n

GC = 128
GN = T // GC
LEVELS = [64, 32, 16, 8, 4, 2, 1]
RC = 64
RN = T // RC
RN_CTX = CTX // RC
INV = [1, 2, 4, 8, 16, 32]
GLA_ORDER = {0: [0, 1, 2, 3, 4, 5], 1: [1, 0, 5, 4, 3, 2]}

C_ID, C_ONE, C_BLK = 0, P, 2 * P
C_LVL = 3 * P
C_AM = C_LVL + 2 * len(LEVELS) * P
C_INV = C_AM + 2 * P
C_INV0T = C_INV + len(INV) * P
C_FG = C_INV0T + P
NCST = C_FG + KT


def ordered(engine, instruction):
    def issue(*args, **kwargs):
        made = instruction(*args, **kwargs)
        engine.drain()
        return made
    return issue


def build_program(nc, x_in, wstream, mstream, par_in, small_in, cst_in, logit_in, cvec_in, out):
    o_spill = nc.dram_tensor("o_spill", (P, HT, T), F32, kind="Internal").ap()
    spill = nc.dram_tensor("x_spill", (P, KT, T), F32, kind="Internal").ap()
    ctx = ExitStack()
    with ctx:
        def sb(name, cols):
            return ctx.enter_context(nc.sbuf_tensor(name, [P, cols], F32))

        def sem(name):
            return ctx.enter_context(nc.semaphore(name))

        ps = ctx.enter_context(nc.psum_tensor("ps", [P, 8, 512], F32))
        XR = sb("XR", KT * T)
        hr_at = nc.sbuf_base
        HR = sb("HR", KT * T)
        mix_at = nc.sbuf_base
        MIX = sb("MIX", KT * T)
        assert nc.sbuf_base == mix_at + KT * T * 4 == hr_at + 2 * KT * T * 4
        HR_R = nc.alloc_sbuf_tensor_at("HR_R", [P, KT * T], F32R, offset=hr_at)
        MIX_R = nc.alloc_sbuf_tensor_at("MIX_R", [P, KT * T], F32R, offset=mix_at)
        AR = sb("AR", 27 * T)
        WR = sb("WR", RING * 1024)
        TMP = sb("TMP", 4096)
        CST = sb("CST", NCST)
        PAR = sb("PAR", NPAR)
        SMALL = sb("SMALL", 3 * 512)
        MOD = sb("MOD", MT * 2)
        COEF = sb("COEF", 9 * KT * 2)
        MTMP = sb("MTMP", RING * 2)
        LG = sb("LG", 8 * 8)
        LBC = sb("LBC", DEPTH * 16)
        LBH = sb("LBH", 4)
        KAX = sb("KAX", 2 * HT)
        EBL = [sb(f"EBL{d}", GN) for d in range(2)]
        PCT = sb("PCT", 2 * HT)
        EPS = sb("EPS", 2)
        eps_rms, eps_gn = EPS[:, 0:1], EPS[:, 1:2]

        X = XR[:, :].rearrange("p (k t) -> p k t", k=KT)
        H = HR[:, :].rearrange("p (k t) -> p k t", k=KT)
        MX = MIX[:, :].rearrange("p (k t) -> p k t", k=KT)
        A = AR[:, :].rearrange("p (k t) -> p k t", t=T)
        W = [WR[:, j * 1024:(j + 1) * 1024] for j in range(RING)]
        TM = TMP[:, 0:5 * T].rearrange("p (k t) -> p k t", t=T)
        ident = CST[:, C_ID:C_ID + P]
        ones = CST[:, C_ONE:C_ONE + P]
        blk = CST[:, C_BLK:C_BLK + P]
        modv = MOD[:, :].rearrange("p (n k s) -> p n k s", n=N_MOD, s=2)
        coef = COEF[:, :].rearrange("p (n q k s) -> p n q k s", n=3, q=3, s=2)
        CBC_FLAT = MIX[:, RING * 1024:RING * 1024 + 2048]
        WM = [MIX[:, j * 1024:(j + 1) * 1024] for j in range(RING)]
        CBC = MIX[:, RING * 1024:RING * 1024 + 2048].rearrange("p (s k) -> p s k", s=2)
        JUNK = TMP[:, 3072:4096]
        HH = MIX_R[:, 0:KT * LAT].rearrange("p (k t) -> p k t", k=KT)
        HL = HR_R[:, :].rearrange("p (k t) -> p k t", k=KT)[:, :, CTX:T]
        WH = [MIX_R[:, KT * LAT + a * HALF * P:KT * LAT + (a + 1) * HALF * P] for a in range(2)]
        WL = [MIX_R[:, KT * LAT + (a + 2) * HALF * P:KT * LAT + (a + 3) * HALF * P] for a in range(2)]

        def par(name, i, n=1):
            a, _ = COLS[name]
            return PAR[:, a + i:a + i + n]

        cst_in_sem = sem("cst_loaded")
        x_loaded = sem("x_loaded")
        par_loaded = sem("par_loaded")
        w_ready = [sem(f"w_ready{j}") for j in range(RING)]
        w_used = sem("w_used")
        dve_setup = sem("dve_setup")
        act_setup = sem("act_setup")
        cvec_loaded = sem("cvec_loaded")
        cvec_ready = sem("cvec_ready")
        m_ready = [sem(f"m_ready{j}") for j in range(RING)]
        wc_ready = sem("wc_ready")
        wc_used = sem("wc_used")
        m_used = sem("m_used")
        spilled = sem("x_spilled")
        reloaded = sem("x_reloaded")
        xr_free = sem("xr_free")
        par_free = sem("par_free")
        out_sem = sem("out_stored")

        class NormSems:
            def __init__(s, n):
                s.sum_ready = sem(f"{n}_sum_ready")
                s.ms_ready = sem(f"{n}_ms_ready")
                s.std_ready = sem(f"{n}_std_ready")
                s.x_scaled = sem(f"{n}_x_scaled")
                s.h_ready = sem(f"{n}_h_ready")
                s.low_ready = sem(f"{n}_low_ready")

        norms = [NormSems(f"norm{i}") for i in range(3)]
        fnorm = NormSems("final")

        class FfnSems:
            def __init__(s, n):
                s.silu_done = sem(f"{n}_silu_done")
                s.act_done = sem(f"{n}_act_done")
                s.res_done = sem(f"{n}_res_done")

        ffns = [FfnSems("ffn1"), FfnSems("ffn2")]
        hg_ev = sem("hg_ev")
        hg_silu = sem("hg_silu")
        rw_ev = sem("rw_ev")
        rw_conv = sem("rw_conv")
        out_res = sem("out_res")

        g_in = sem("gla_in")
        g_vt_ps = sem("gla_vt_ps")
        g_vt = sem("gla_vt")
        g_lb = sem("gla_lb")
        g_gate = sem("gla_gate")
        g_w = sem("gla_w")
        g_f = sem("gla_f")
        g_b = sem("gla_b")
        g_kx = sem("gla_kx")
        g_bl = sem("gla_bl")
        g_qe = sem("gla_qe")
        g_k = sem("gla_k")
        g_ke = sem("gla_ke")
        g_q = sem("gla_q")
        g_kt_ps = sem("gla_kt_ps")
        g_kt = sem("gla_kt")
        g_u = sem("gla_u")
        g_s = sem("gla_s")
        g_dx = sem("gla_dx")
        g_ex = sem("gla_ex")
        g_z = sem("gla_z")
        g_att_ps = sem("gla_att_ps")
        g_att = sem("gla_att")
        g_o_ps = sem("gla_o_ps")
        g_o = sem("gla_o")
        on_sq = sem("on_sq")
        on_ps = sem("on_ps")
        on_std = sem("on_std")
        on_rec = sem("on_rec")
        on_done = sem("on_done")

        p_th = sem("rp_tanh")
        p_mm = sem("rp_mm")
        p_ev = sem("rp_ev")
        p_sq = sem("rp_sq")
        p_ss = sem("rp_ss")
        p_mx = sem("rp_mx")
        p_sd = sem("rp_sd")
        p_kn = sem("rp_kn")

        r_cum = sem("rk_cum")
        r_exp = sem("rk_exp")
        r_bk = sem("rk_bk")
        r_kr = sem("rk_kr")
        r_v = sem("rk_v")
        r_ve = sem("rk_ve")
        r_bt = sem("rk_bt")
        r_bte = sem("rk_bte")
        r_am_ps = sem("rk_am_ps")
        r_am = sem("rk_am")
        r_r = sem("rk_r")
        r_re = sem("rk_re")
        r_t = sem("rk_t")
        r_w = sem("rk_w")
        r_xy = sem("rk_xy")
        r_xye = sem("rk_xye")
        r_sa = sem("rk_sa")
        r_sae = sem("rk_sae")
        r_s = sem("rk_s")
        r_se = sem("rk_se")
        r_y = sem("rk_y")
        r_ye = sem("rk_ye")
        o_spilled = sem("o_spilled")
        q_b = sem("rq_b")
        q_e = sem("rq_e")
        q_c = sem("rq_c")
        q_d = sem("rq_d")
        q_std = sem("rq_std")
        q_a = sem("rq_a")
        q_v = sem("rq_v")
        q_ve = sem("rq_ve")
        q_g = sem("rq_g")
        q_f = sem("rq_f")

        def slot_value(l, s, extra=0):
            return (l * (SLOTS // RING) + s // RING + extra + 1) * 16

        def halves(b, lat=False):
            both = ((slice(0, CTX), ps[:, b, 0:CTX]), (slice(CTX, T), ps[:, b + 1, 0:LAT]))
            return both[1:] if lat else both

        def span(lat):
            return slice(CTX if lat else 0, T)

        def xt(i):
            return XR[:, i * T:(i + 1) * T]

        G_QS, G_KS, G_B = [xt(0), xt(1)], [xt(2), xt(3)], [xt(4), xt(5)]
        G_KE, G_KET, G_IS, G_VT = xt(6), MX[:, 4], MX[:, 5], MX[:, 6]
        G_TA, G_TB, G_RA, G_RB = xt(7), MX[:, 7], A[:, 26], TM[:, 4]
        G_QE = [A[:, 20], A[:, 21]]
        G_ATT = [A[:, 22], A[:, 23]]
        G_S = [A[:, 24], A[:, 25]]
        G_E = [TM[:, 0], TM[:, 1]]
        G_Z = [TM[:, 2], TM[:, 3]]

        at = [0]

        def rb(n):
            a = at[0]
            at[0] += n
            assert at[0] <= KT * T
            return XR[:, a:a + n]

        R_UI = rb(1024).rearrange("p (h c) -> p h c", h=8)
        R_AKK = rb(1024).rearrange("p (h c) -> p h c", h=8)
        R_AMR = rb(1024).rearrange("p (d h c) -> p d h c", d=2, h=8)
        R_BKT = rb(1024).rearrange("p (d j c) -> p d j c", d=2, j=HT)
        R_SAV = rb(1024).rearrange("p (d h c) -> p d h c", d=2, h=8)
        R_STF = rb(1024)
        R_ST = R_STF.rearrange("p (d j c) -> p d j c", d=2, j=HT)

        R_KR = TMP[:, 0:1024].rearrange("p (d j a c) -> p d j a c", d=2, j=HT, a=2)
        R_BK = TMP[:, 1024:2048].rearrange("p (d j a c) -> p d j a c", d=2, j=HT, a=2)
        R_X = TMP[:, 2048:3072].rearrange("p (h c) -> p h c", h=8)
        R_Y = TMP[:, 3072:4096].rearrange("p (h c) -> p h c", h=8)
        R_W = AR[:, 12 * T:12 * T + 1024].rearrange("p (h c) -> p h c", h=8)
        R_RS = AR[:, 12 * T + 1024:14 * T].rearrange("p (h c) -> p h c", h=8)
        R_EI = SMALL[:, 0:512].rearrange("p (d j c) -> p d j c", d=2, j=HT)
        R_T1 = SMALL[:, 512:1024].rearrange("p (d j c) -> p d j c", d=2, j=HT)
        R_EP = MIX[:, 0:2 * HT * (RC + 1)].rearrange("p (d j c) -> p d j c", d=2, j=HT)
        R_VS = MIX[:, 1024:1536].rearrange("p (h c) -> p h c", h=8)

        R_r, R_k, R_v, R_kk = A[:, 0:4], A[:, 4:8], A[:, 8:12], A[:, 15:19]
        R_a = [A[:, 19:23], A[:, 23:27]]
        R_lw = [H[:, 0:4], H[:, 4:8]]
        YB = MX[:, HT:2 * HT]
        Y_BONUS = [H[:, j] for j in range(HT)]
        Y_SQ = [H[:, HT + j] for j in range(HT)]

        def chunked(t):
            return t.rearrange("p (c t) -> p c t", t=GC)

        settled = {}

        def settle(engine, name):
            if name not in settled:
                settled[name] = sem(f"{name}_settled")
            engine.sem_inc(settled[name], 1)

        block = ctx.enter_context(nc.Block())

        @block.sync
        def _(sp):
            for j in range(RING):
                sp.dma_start(W[j], wstream[j]).then_inc(w_ready[j], 16)
            with sp.Fori(1, DEPTH * SLOTS // RING) as g:
                for j in range(RING):
                    sp.wait_ge(w_used, g * RING + (j + 1 - RING))
                    sp.dma_start(W[j], wstream[g * RING + j]).then_inc(w_ready[j], 16)
            sp.wait_ge(fnorm.h_ready, KT)
            sp.dma_start(out, H[:, :, CTX:T]).then_inc(out_sem, 16)
            sp.wait_ge(out_sem, 16)

        @block.gpsimd
        def _(pool):
            pool.dma_start(CST[:, :], cst_in).then_inc(cst_in_sem, 16)
            pool.dma_start(LG[:, 0:16], logit_in).then_inc(cst_in_sem, 16)

            def parameters(l):
                pool.dma_start(PAR[:, :], par_in[l]).then_inc(par_loaded, 16)
                pool.dma_start(SMALL[:, :], small_in[l]).then_inc(par_loaded, 16)

            p_copy, p_tt, p_ts = (ordered(pool, f) for f in (pool.tensor_copy, pool.tensor_tensor,
                                                             pool.tensor_scalar))

            def split(l, n, up):
                with pool.Fori(0, UPS // RING) as i:
                    for j in range(RING):
                        pool.wait_ge(w_ready[j], slot_value(l, up, i))
                        for a in range(2):
                            pool.wait_ge(wc_used, ((l * 2 + n) * UPS + i * RING + j) * 2 + (a + 1))
                            settle(pool, "pool")
                            half = W[j][:, a * HALF * P:(a + 1) * HALF * P]
                            p_copy(WH[a], half)
                            p_tt(WL[a], half, WH[a].bitcast(F32), ALU.subtract).then_inc(wc_ready, 1)

            def condition():
                pool.dma_start(CBC_FLAT, cvec_in).then_inc(cvec_loaded, 16)

            def modulation(l, i0, i1):
                with pool.Fori(i0, i1) as i:
                    for j in range(RING):
                        g = l * MG + i
                        pool.wait_ge(m_used, g * RING + (j + 1))
                        settle(pool, "pool")
                        pool.dma_start(WM[j], mstream[g * RING + j]).then_inc(m_ready[j], 16)

            def gate(l, h, d):
                v = (l * HT + h) * 2 + d
                z = A[:, bass.ds(h + (4 + 4 * d), 1)].rearrange("p a t -> p (a t)")
                pool.wait_ge(g_gate, v + 1)
                settle(pool, "pool")
                p_tt(G_TA, G_TA, G_RA, ALU.add)
                p_tt(G_RB, G_RB, G_TB, ALU.add)
                p_tt(G_TB, G_TA, z, ALU.add).then_inc(g_w, 1)
                p_tt(G_RB, G_RB, G_TA, ALU.subtract).then_inc(g_f, 1)
                last_t = 0 if d else GC - 1
                b3 = chunked(G_B[d])
                pool.wait_ge(g_b, v + 1)
                settle(pool, "pool")
                p_tt(chunked(G_TA), b3[:, :, last_t:last_t + 1].to_broadcast([P, GN, GC]), b3,
                     ALU.subtract).then_inc(g_bl, 1)
                pool.wait_ge(g_kx, v + 1)
                settle(pool, "pool")
                p_ts(G_KS[d], G_KS[d], LBH[:, 2 + d:3 + d], None, ALU.mult).then_inc(g_k, 1)
                pool.wait_ge(g_qe, v + 1)
                settle(pool, "pool")
                p_copy(EBL[d][:, :].unsqueeze(2), chunked(G_QE[d])[:, :, last_t:last_t + 1])
                p_tt(G_KE, G_KE, G_KS[d], ALU.mult).then_inc(g_ke, 1)
                p_tt(G_QE[d], G_QE[d], G_QS[d], ALU.mult).then_inc(g_q, 1)

            def layer(l, last):
                pool.wait_ge(m_used, (l * MG + MG_NEXT) * RING + RING)
                settle(pool, "pool")
                split(l, 0, S_UP1)
                pool.wait_ge(wc_used, (l * 2 + 1) * UPS * 2 + 2)
                settle(pool, "pool")
                condition()
                modulation(l, MG_NEXT, MG)
                pool.wait_ge(norms[1].h_ready, (l + 1) * KT)
                settle(pool, "pool")
                pool.dma_start(spill, X).then_inc(spilled, 16)
                with pool.Fori(0, HT) as h:
                    for d in range(2):
                        gate(l, h, d)
                sp = span(last)
                for h in range(HT):
                    pool.wait_ge(on_rec, l * HT + h + 1)
                    settle(pool, "pool")
                    p_ts(MX[:, h, sp], MX[:, h, sp], par("ogain", h), None, ALU.mult)
                    p_tt(MX[:, h, sp], MX[:, h, sp], xt(h)[:, sp], ALU.mult)
                    done = p_tt(MX[:, h, sp], MX[:, h, sp], A[:, 16 + h, sp], ALU.mult)
                done.then_inc(on_done, 1)
                pool.wait_ge(on_done, l + 1)
                settle(pool, "pool")
                pool.dma_start(o_spill, MX[:, 0:HT]).then_inc(o_spilled, 16)
                pool.wait_ge(xr_free, l + 1)
                settle(pool, "pool")
                pool.dma_start(MX[:, 0:HT], o_spill).then_inc(reloaded, 16)
                pool.dma_start(X, spill).then_inc(reloaded, 16)
                if not last:
                    pool.wait_ge(par_free, l + 1)
                    settle(pool, "pool")
                    parameters(l + 1)
                pool.wait_ge(w_used, l * SLOTS + (S_OUT + KT))
                settle(pool, "pool")
                split(l, 1, S_UP2)
                if not last:
                    pool.wait_ge(wc_used, (l * 2 + 2) * UPS * 2 + 2)
                    settle(pool, "pool")
                    condition()
                    modulation(l + 1, 0, MG_NEXT)

            pool.dma_start(X, x_in).then_inc(x_loaded, 16)
            parameters(0)
            condition()
            modulation(0, 0, MG_NEXT)
            with pool.Fori(0, DEPTH - 1) as l:
                layer(l, False)
            layer(DEPTH - 1, True)

        @block.tensor
        def _(pe):
            def tile_products(b, j, rhs, k0, nk, start, stop, lat=False, ready=None):
                for k in range(nk):
                    if ready is not None:
                        pe.wait_ge(ready[0], ready[1] + (k + 1))
                    for sl, dst in halves(b, lat):
                        last = pe.matmul(dst, W[j][:, k * P:(k + 1) * P], rhs[:, k0 + k, sl],
                                         start=start and k == 0, stop=stop and k == nk - 1)
                return last

            def norm(l, s, lat=False):
                pe.wait_ge(s.sum_ready, l + 1)
                for sl, dst in halves(0, lat):
                    last = pe.matmul(dst, ones, TM[:, 2, sl], start=True, stop=True)
                last.then_inc(s.ms_ready, 1)

            def ffn(l, n, up, dn, lat=False):
                s = ffns[n]
                def up_product(slot, b, j, first):
                    for k in range(KT):
                        a, o = k // HALF, k % HALF * P
                        if first:
                            pe.wait_ge(norms[2 * n].h_ready, l * KT + (k + 1))
                            pe.wait_ge(norms[2 * n].low_ready, l * KT + (k + 1))
                        if k % HALF == 0:
                            pe.wait_ge(wc_ready, ((l * 2 + n) * UPS + slot) * 2 + (a + 1))
                        if not lat:
                            last = pe.matmul(ps[:, b, 0:CTX], W[j][:, k * P:(k + 1) * P], H[:, k, 0:CTX],
                                             start=k == 0, stop=k == KT - 1)
                            if k == KT - 1:
                                last.then_inc(w_used, 1)
                        parts = ((WH, HH[:, k]), (WH, HL[:, k]), (WL, HH[:, k]))
                        for m, (w, h) in enumerate(parts):
                            last = pe.matmul(ps[:, b + 1, 0:LAT], w[a][:, o:o + P], h,
                                             start=k == 0 and m == 0, stop=k == KT - 1 and m == 2)
                            if lat and k == KT - 1 and m == 0:
                                last.then_inc(w_used, 1)
                        if k % HALF == HALF - 1:
                            last.then_inc(wc_used, 1)

                with pe.Fori(0, FT // 2) as i:
                    for j in range(2):
                        pe.wait_ge(s.act_done, l * FT + i * 2 + (j + 1))
                        for a in range(2):
                            pe.wait_ge(w_ready[2 * j + a], slot_value(l, up, i))
                            up_product(i * RING + (2 * j + a), 4 * j + 2 * a, 2 * j + a, j == 0 and a == 0)
                pe.wait_ge(s.act_done, (l + 1) * FT + 2)
                settle(pe, "pe")
                with pe.Fori(0, 2) as g:
                    for m in range(4):
                        pe.wait_ge(s.res_done, l * KT + g * 4 + (m + 1))
                        k0 = 0
                        for r, nk in enumerate(DOWN_K):
                            t = 3 * m + r
                            pe.wait_ge(w_ready[t % RING], slot_value(l, dn + t, g * 3))
                            last = tile_products(2 * m, t % RING, A, k0, nk, r == 0, r == 2, lat)
                            last.then_inc(w_used, 1)
                            k0 += nk

            def project(l, first, n, n4, rhs, ev, lat=False, ready=None):
                def group(i, k):
                    for j in range(k):
                        pe.wait_ge(ev, l * n + i * RING + (j + 1))
                        pe.wait_ge(w_ready[j], slot_value(l, first, i))
                        pad = 0
                        if j == k - 1 and k < RING:
                            pad = RING - k
                            pe.wait_ge(w_ready[RING - 1], slot_value(l, first, i))
                        last = tile_products(2 * j, j, rhs, 0, KT, True, True, lat, ready if j == 0 else None)
                        last.then_inc(w_used, 1 + pad)
                with pe.Fori(0, n4) as i:
                    group(i, RING)
                if n > n4 * RING:
                    group(n4, n - n4 * RING)

            def three(b, c):
                return ps[:, b + c // 3, (c % 3) * GC:(c % 3 + 1) * GC]

            def gla(l):
                pe.wait_ge(hg_silu, l + 1)
                pe.wait_ge(hg_ev, (l + 1) * HG_T + 4)
                settle(pe, "pe")

                def scores(v, d):
                    pe.wait_ge(g_k, v + 1)
                    for c in range(GN):
                        sl = slice(c * GC, (c + 1) * GC)
                        last = pe.matmul(three(0, c), G_KS[d][:, sl], G_QS[d][:, sl], start=True, stop=True)
                    last.then_inc(g_att_ps, 1)
                    pe.wait_ge(g_ke, v + 1)
                    for c in range(GN):
                        last = pe.transpose(three(4, c), G_KE[:, c * GC:(c + 1) * GC], ident)
                    last.then_inc(g_kt_ps, 1)

                def unit(u, d, more):
                    v = u * 2 + d
                    pe.wait_ge(g_kt, v + 1)
                    if d == 0:
                        pe.wait_ge(g_in, u + 1)
                        for c in range(GN):
                            last = pe.transpose(three(4, c), G_IS[:, c * GC:(c + 1) * GC], ident)
                        last.then_inc(g_vt_ps, 1)
                        pe.wait_ge(g_vt, u + 1)
                    for c in range(GN):
                        sl = slice(c * GC, (c + 1) * GC)
                        last = pe.matmul(three(4, c), G_KET[:, sl], G_VT[:, sl], start=True, stop=True)
                    last.then_inc(g_u, 1)
                    for n in range(len(LEVELS)):
                        b = 2 * ((n + 1) % 2)
                        pe.wait_ge(g_z, v * 7 + (n + 1))
                        if n >= 1:
                            pe.wait_ge(g_att, v * 8 + n)
                        for c in range(GN):
                            sl = slice(c * GC, (c + 1) * GC)
                            z = G_Z[n % 2][:, sl]
                            last = pe.matmul(three(b, c), z, z, start=True, stop=True)
                        last.then_inc(g_att_ps, 1)
                    pe.wait_ge(g_att, v * 8 + 7)
                    pe.wait_ge(g_s, v + 1)
                    if more:
                        scores(v + 1, 1 - d)
                    pe.wait_ge(g_att, v * 8 + 8)
                    pe.wait_ge(g_q, v + 1)
                    for c in range(GN):
                        sl = slice(c * GC, (c + 1) * GC)
                        first = GLA_ORDER[d][0]
                        last = pe.matmul(three(6, c), G_VT[:, sl], G_ATT[d][:, sl],
                                         start=d == 0 and c % 3 == 0, stop=d == 1 and c == first,
                                         skip_group_check=True)
                        if c != first:
                            last = pe.matmul(three(6, c), G_S[d][:, sl], G_QE[d][:, sl],
                                             start=False, stop=d == 1, skip_group_check=True)
                    if d == 1:
                        last.then_inc(g_o_ps, 1)
                        pe.wait_ge(g_o, u + 1)

                scores(l * HT * 2, 0)
                with pe.Fori(0, HT - 1) as h:
                    unit(l * HT + h, 0, True)
                    unit(l * HT + h, 1, True)
                unit(l * HT + (HT - 1), 0, True)
                unit(l * HT + (HT - 1), 1, False)

            def o_norm(l, lat):
                for h in range(HT):
                    pe.wait_ge(on_sq, l * HT + h + 1)
                    for sl, dst in halves(2 * h, lat):
                        last = pe.matmul(dst, ones, TM[:, h, sl], start=True, stop=True)
                    last.then_inc(on_ps, 1)

            def rwkv_prep(l):
                for j in range(HT):
                    pe.wait_ge(p_sq, l * HT + j + 1)
                    for sl, dst in halves(2 * j):
                        last = pe.matmul(dst, blk, TM[:, j, sl], start=True, stop=True)
                    last.then_inc(p_ss, 1)
                pe.wait_ge(p_mx, (l + 1) * HT)
                pe.wait_ge(p_th, l + 1)
                n = 0
                for j in range(HT):
                    for q in range(2):
                        for d in range(2):
                            pe.wait_ge(p_ev, l * 16 + n + 1)
                            hf = slice(64 * d, 64 * d + 64)
                            for sl, dst in halves(4 * d + 2 * q):
                                last = pe.matmul(dst, SMALL[hf, q * 512 + j * P:q * 512 + (j + 1) * P],
                                                 A[hf, 12 + q, sl], start=True, stop=True)
                            last.then_inc(p_mm, 1)
                            n += 1
                pe.wait_ge(p_ev, l * 16 + 16 + 4)

            def rwkv(l):
                hd = [slice(0, 64), slice(64, 128)]

                def flat(t):
                    return t.rearrange("p a c -> p (a c)")

                def group(b, g, lhs, rhs, done):
                    for k in range(4):
                        h = 4 * g + k
                        last = pe.matmul(ps[:, b + g, k * P:(k + 1) * P], lhs[:, h], rhs[:, h],
                                         start=True, stop=True)
                    if done is not None:
                        last.then_inc(done, 1)

                def products(u):
                    pe.wait_ge(r_bk, u + 1)
                    pe.wait_ge(r_kr, u + 1)
                    for d in range(2):
                        for j in range(HT):
                            for e in range(2):
                                last = pe.matmul(ps[:, 2 * d + e, j * P:(j + 1) * P],
                                                 flat(R_BK[hd[e], d, j]), flat(R_KR[hd[e], d, j]),
                                                 start=True, stop=True)
                    last.then_inc(r_am_ps, 1)

                def transposed_bk():
                    for d in range(2):
                        for j in range(HT):
                            last = pe.transpose(ps[:, 4 + d, j * P:(j + 1) * P], flat(R_BK[:, d, j]), ident)
                    last.then_inc(r_bt, 1)

                def step(u, more):
                    pe.wait_ge(r_se, u + 1)
                    for d in range(2):
                        for j in range(HT):
                            last = pe.matmul(ps[hd[1 - d], 6, j * P:(j + 1) * P], R_T1[:, d, j], ident,
                                             start=True, stop=True)
                    last.then_inc(r_v, 1)
                    pe.wait_ge(r_am, u + 1)
                    for g in range(2):
                        for k in range(4):
                            last = pe.matmul(ps[:, g, k * P:(k + 1) * P], R_UI[:, 4 * g + k], ident,
                                             start=True, stop=True)
                        last.then_inc(r_t, 1)
                    pe.wait_ge(r_ve, u + 1)
                    for h in range(8):
                        pe.matmul(ps[:, 6, h * 64:(h + 1) * 64], R_AKK[:, h], R_VS[:, h],
                                  start=h == 0, stop=False, skip_group_check=True)
                    for d in range(2):
                        for j in range(HT):
                            last = pe.matmul(ps[hd[d], 6, j * P:(j + 1) * P], R_KR[:, d, j, 0], R_ST[:, d, j],
                                             start=False, stop=True, skip_group_check=True)
                    last.then_inc(r_r, 1)
                    for n in range(1, len(INV)):
                        for g in range(2):
                            if n == 1:
                                pe.wait_ge(r_w, u * 12 + (g + 1))
                            else:
                                pe.wait_ge(r_xye, u * 10 + (2 * (n - 2) + g + 1))
                            group(0, g, R_UI, R_X, r_t)
                        if n == 1:
                            pe.wait_ge(r_ye, u + 1)
                            for d in range(2):
                                for j in range(HT):
                                    o = (d * HT + j) * 64
                                    pe.matmul(ps[:, 7, o:o + 64], R_ST[:, d, j], R_KR[:, d, j, 1],
                                              start=d == 0 and j == 0, stop=False, skip_group_check=True)
                            pe.wait_ge(r_bte, u + 1)
                        for g in range(2):
                            pe.wait_ge(r_w, u * 12 + (2 * n + g + 1))
                            if n < len(INV) - 1:
                                group(2, g, R_Y, R_W, None)
                            group(4, g, R_W, R_Y, r_xy)
                    if more:
                        products(u + 1)
                    pe.wait_ge(r_re, u + 1)
                    pe.wait_ge(r_xye, (u + 1) * 10)
                    for h in range(8):
                        last = pe.matmul(ps[:, 6, h * 64:(h + 1) * 64], R_Y[:, h], R_RS[:, h],
                                         start=True, stop=True)
                    last.then_inc(r_sa, 1)
                    if more:
                        transposed_bk()
                    pe.wait_ge(r_sae, u + 1)
                    for d in range(2):
                        for j in range(HT):
                            o = (d * HT + j) * 64
                            for e in range(2):
                                last = pe.matmul(ps[hd[e], 6, o:o + 64], R_BKT[:, d, j, e * 64:(e + 1) * 64],
                                                 R_SAV[:, d, 2 * j + e], start=True, stop=True)
                    last.then_inc(r_s, 1)
                    for d in range(2):
                        for j in range(HT):
                            o = (d * HT + j) * 64
                            for e in range(2):
                                last = pe.matmul(ps[hd[e], 7, o:o + 64], R_SAV[:, d, 2 * j + e],
                                                 R_AMR[:, d, 2 * j + e], start=False, stop=True,
                                                 skip_group_check=True)
                    last.then_inc(r_y, 1)

                pe.wait_ge(p_kn, (l + 1) * HT)
                settle(pe, "pe")
                products(l * RN)
                transposed_bk()
                with pe.Fori(0, RN - 1) as i:
                    step(l * RN + i, True)
                step(l * RN + (RN - 1), False)

            def y_post(l, lat):
                def per_head(j, lhs, rhs):
                    for sl, dst in halves(2 * j, lat):
                        last = pe.matmul(dst, lhs, rhs[:, sl], start=True, stop=True)
                    return last

                pe.wait_ge(r_ye, (l + 1) * RN + 1)
                for j in range(HT):
                    per_head(j, blk, YB[:, j]).then_inc(q_b, 1)
                for j in range(HT):
                    pe.wait_ge(q_c, l * HT + j + 1)
                    per_head(j, blk, Y_SQ[j]).then_inc(q_d, 1)
                for j in range(HT):
                    pe.wait_ge(q_std, l * HT + j + 1)
                    pe.wait_ge(q_a, l * HT + j + 1)
                    per_head(j, blk, Y_BONUS[j]).then_inc(q_v, 1)
                for j in range(HT):
                    pe.wait_ge(q_ve, l * HT + j + 1)
                    per_head(j, SMALL[:, 1024 + j * P:1024 + (j + 1) * P], A[:, 14]).then_inc(q_g, 1)

            def layer(l, last):
                norm(l, norms[0])
                ffn(l, 0, S_UP1, S_DN1)
                norm(l, norms[1])
                project(l, S_HG, HG_T, HG_T // RING, H, hg_ev, ready=(norms[1].h_ready, l * KT))
                gla(l)
                o_norm(l, last)
                pe.wait_ge(on_std, (l + 1) * HT)
                settle(pe, "pe")
                project(l, S_RW, RW_T, RW_T // RING, H, rw_ev)
                pe.wait_ge(par_loaded, 32 * (l + 1))
                rwkv_prep(l)
                rwkv(l)
                y_post(l, last)
                pe.wait_ge(q_f, (l + 1) * HT)
                pe.wait_ge(reloaded, 32 * (l + 1))
                settle(pe, "pe")
                project(l, S_OUT, KT, KT // RING, MX, out_res, last)
                norm(l, norms[2], last)
                ffn(l, 1, S_UP2, S_DN2, last)

            pe.wait_ge(cst_in_sem, 32)
            pe.wait_ge(dve_setup, 1)
            settle(pe, "pe")
            with pe.Fori(0, DEPTH - 1) as l:
                layer(l, False)
            layer(DEPTH - 1, True)
            norm(0, fnorm, True)

        @block.scalar
        def _(act):
            activation = ordered(act, act.activation)

            def norm(l, s, n, lat=False):
                act.wait_ge(s.ms_ready, l + 1)
                for sl, src in halves(0, lat):
                    activation(TM[:, 3, sl], src, ACT.Sqrt, bias=eps_rms, scale=1.0 / D).then_inc(s.std_ready, 1)
                if n is not None:
                    for k in range(KT):
                        act.wait_ge(s.x_scaled, l * KT + k + 1)
                        for sl, _ in halves(0, lat):
                            q = 1 if sl.start == 0 else 0
                            dst = HH[:, k] if q == 0 and n != 1 else H[:, k, sl]
                            last = activation(dst, H[:, k, sl], ACT.Identity, bias=coef[:, n, 1, k, q:q + 1])
                        last.then_inc(s.h_ready, 1)

            def condition(count):
                act.wait_ge(cvec_loaded, count * 16)
                activation(CBC, CBC, ACT.Silu).then_inc(cvec_ready, 1)

            def ffn(l, n, lat=False):
                s = ffns[n]
                with act.Fori(0, FT // 2) as i:
                    for j in range(2):
                        act.wait_ge(wc_used, ((l * 2 + n) * UPS + i * RING + 2 * (j + 1)) * 2 + 2)
                        act.wait_ge(s.act_done, l * FT + i * 2 + (j + 1))
                        for sl, src in halves(4 * j, lat):
                            last = activation(TM[:, j, sl], src, ACT.Silu)
                        last.then_inc(s.silu_done, 1)
                if not lat:
                    settle(act, "act")
                    condition(l * 2 + n + 2)

            def gla(l, lat):
                for t in (0, 1, 2, 3, 16, 17, 18, 19):
                    last = activation(A[:, t], A[:, t], ACT.Silu)
                last.then_inc(hg_silu, 1)
                act.wait_ge(spilled, 16 * (l + 1))
                settle(act, "act")

                def arena(i):
                    return A[:, bass.ds(i, 1)].rearrange("p a t -> p (a t)")

                def gate_q(v, h, d):
                    if d == 0:
                        act.wait_ge(g_lb, l * HT + h + 1)
                    activation(G_QS[d], arena(h), ACT.Copy)
                    activation(G_TA, arena(h + (4 + 4 * d)), ACT.Abs)
                    activation(G_TB, arena(h + (4 + 4 * d)), ACT.Abs, bias=LBH[:, d:d + 1], scale=-1.0)

                def gate_relu(v, h, d):
                    activation(G_RA, arena(h + (4 + 4 * d)), ACT.Relu, scale=-1.0)
                    activation(G_RB, arena(h + (4 + 4 * d)), ACT.Relu, bias=LBH[:, d:d + 1], scale=-1.0)
                    if d == 0:
                        activation(G_IS, arena(h + 12), ACT.Copy).then_inc(g_in, 1)

                def gate_exp(v, h, d):
                    activation(G_TA, G_TA, ACT.Exp, scale=-1.0)
                    activation(G_TB, G_TB, ACT.Exp, scale=-1.0)

                def gate_ln(v, h, d):
                    activation(G_TA, G_TA, ACT.Ln, bias=1.0)
                    activation(G_TB, G_TB, ACT.Ln, bias=1.0).then_inc(g_gate, 1)

                def gate_key(v, h, d):
                    act.wait_ge(g_w, v + 1)
                    activation(G_KS[d], G_TB, ACT.Exp, scale=-1.0).then_inc(g_kx, 1)

                def gate_decay(v, h, d):
                    act.wait_ge(g_bl, v + 1)
                    activation(G_QE[d], G_B[d], ACT.Exp)
                    activation(G_KE, G_TA, ACT.Exp).then_inc(g_qe, 1)

                def keys_out(v):
                    act.wait_ge(g_kt_ps, v + 1)
                    activation(G_KET.rearrange("p (a t) -> p a t", a=2), ps[:, 4:6, 0:384],
                               ACT.Copy).then_inc(g_kt, 1)

                gate = (gate_q, gate_relu, gate_exp, gate_ln, gate_key, gate_decay)

                def unit(h, d, nxt):
                    u = l * HT + h
                    v = u * 2 + d
                    if d == 0:
                        act.wait_ge(g_vt_ps, u + 1)
                        activation(G_VT.rearrange("p (a t) -> p a t", a=2), ps[:, 4:6, 0:384],
                                   ACT.Copy).then_inc(g_vt, 1)
                    for n in range(len(LEVELS)):
                        act.wait_ge(g_dx, v * 7 + (n + 1))
                        activation(G_E[n % 2], G_E[n % 2], ACT.Exp).then_inc(g_ex, 1)
                        if nxt is not None and n < len(gate):
                            gate[n](v + 1, *nxt)
                    if nxt is not None:
                        keys_out(v + 1)
                    if d == 1:
                        act.wait_ge(g_o_ps, u + 1)
                        activation(MX[:, bass.ds(h, 1)].rearrange("p b (a t) -> p (b a) t", a=2),
                                   ps[:, 6:8, 0:384], ACT.Copy).then_inc(g_o, 1)

                v0 = l * HT * 2
                for part in gate:
                    part(v0, 0, 0)
                keys_out(v0)
                with act.Fori(0, HT - 1) as h:
                    unit(h, 0, (h, 1))
                    unit(h, 1, (h + 1, 0))
                unit(HT - 1, 0, (HT - 1, 1))
                unit(HT - 1, 1, None)
                for h in range(HT):
                    activation(TM[:, h, span(lat)], MX[:, h, span(lat)], ACT.Square).then_inc(on_sq, 1)
                for h in range(HT):
                    act.wait_ge(on_ps, l * HT + h + 1)
                    for sl, src in halves(2 * h, lat):
                        last = activation(xt(h)[:, sl], src, ACT.Sqrt, bias=eps_rms, scale=1.0 / P)
                    last.then_inc(on_std, 1)

            def project_hg(l):
                with act.Fori(0, HG_T // RING) as i:
                    for j in range(RING):
                        act.wait_ge(w_used, l * SLOTS + i * RING + (S_HG + j + 1))
                        dst = A[:, bass.ds(i * RING + j, 1)].rearrange("p a t -> p (a t)")
                        for sl, src in halves(2 * j):
                            last = activation(dst[:, sl], src, ACT.Copy)
                        last.then_inc(hg_ev, 1)

            def project_rw(l):
                def group(i, k):
                    for j in range(k):
                        act.wait_ge(w_used, l * SLOTS + i * RING + (S_RW + j + 1))
                        act.wait_ge(rw_conv, l * RW_T + i * RING + (j + 1))
                        for sl, src in halves(2 * j):
                            last = activation(TM[:, j % 2, sl], src, ACT.Copy)
                        last.then_inc(rw_ev, 1)
                with act.Fori(0, RW_T // RING) as i:
                    group(i, RING)
                group(RW_T // RING, RW_T % RING)

            def rwkv_prep(l):
                for j in range(HT):
                    act.wait_ge(p_mx, l * HT + j + 1)
                    activation(TM[:, j], TM[:, j], ACT.Sqrt).then_inc(p_sd, 1)
                act.wait_ge(rw_conv, (l + 1) * RW_T + 2)
                activation(A[:, 12], A[:, 12], ACT.Tanh)
                activation(A[:, 14], A[:, 14], ACT.Sigmoid).then_inc(p_th, 1)
                n = 0
                for j in range(HT):
                    for q in range(2):
                        for d in range(2):
                            act.wait_ge(p_mm, l * 16 + n + 1)
                            dst = (R_lw, R_a)[q][d][:, j]
                            bias = par(("w0", "a0")[q], d * HT + j)
                            for sl, src in halves(4 * d + 2 * q):
                                last = activation(dst[:, sl], src, ACT.Sigmoid, bias=bias)
                            last.then_inc(p_ev, 1)
                            n += 1

            def rwkv(l):
                def heads(t):
                    return t.rearrange("p (h c) -> p h c", h=8)

                def exponentials(u):
                    act.wait_ge(r_cum, u + 1)
                    for d in range(2):
                        activation(R_EP[:, d, :, 1 - d:1 - d + RC], R_T1[:, d], ACT.Exp, scale=-RSQRT_E)
                        last = activation(R_EI[:, d], R_T1[:, d], ACT.Exp, scale=RSQRT_E)
                    last.then_inc(r_exp, 1)

                def step(u, more):
                    act.wait_ge(r_v, u + 1)
                    v_ps = heads(ps[:, 6, :])
                    activation(R_VS, v_ps, ACT.Copy)
                    activation(R_SAV[64:128, 0], v_ps[64:128], ACT.Copy)
                    activation(R_SAV[0:64, 1], v_ps[0:64], ACT.Copy).then_inc(r_ve, 1)
                    act.wait_ge(r_bt, u + 1)
                    activation(R_BKT, ps[:, 4:6, :].rearrange("p d (j c) -> p d j c", j=HT),
                               ACT.Copy).then_inc(r_bte, 1)
                    act.wait_ge(r_r, u + 1)
                    activation(R_RS, heads(ps[:, 6, :]), ACT.Copy, scale=-1.0).then_inc(r_re, 1)
                    for n in range(1, len(INV)):
                        for g in range(2):
                            act.wait_ge(r_xy, u * 10 + (2 * (n - 1) + g + 1))
                            q = slice(4 * g, 4 * g + 4)
                            if n < len(INV) - 1:
                                activation(R_X[:, q], ps[:, 2 + g, :].rearrange("p (h c) -> p h c", h=4), ACT.Copy)
                            activation(R_Y[:, q], ps[:, 4 + g, :].rearrange("p (h c) -> p h c", h=4),
                                       ACT.Copy).then_inc(r_xye, 1)
                        if n == 1 and more:
                            exponentials(u + 1)
                    act.wait_ge(r_sa, u + 1)
                    sa_ps = heads(ps[:, 6, :])
                    activation(R_SAV[0:64, 0], sa_ps[0:64], ACT.Copy)
                    activation(R_SAV[64:128, 1], sa_ps[64:128], ACT.Copy).then_inc(r_sae, 1)

                act.wait_ge(r_cum, l * RN + 1)
                settle(act, "act")
                exponentials(l * RN)
                with act.Fori(0, RN - 1) as i:
                    step(l * RN + i, True)
                step(l * RN + (RN - 1), False)

            def y_post(l, lat):
                sp = span(lat)
                for j in range(HT):
                    act.wait_ge(q_e, l * HT + j + 1)
                    activation(Y_SQ[j][:, sp], YB[:, j, sp], ACT.Square).then_inc(q_c, 1)
                for j in range(HT):
                    act.wait_ge(q_d, l * HT + j + 1)
                    for sl, src in halves(2 * j, lat):
                        last = activation(TM[:, j, sl], src, ACT.Sqrt, bias=eps_gn, scale=1.0 / 64)
                    last.then_inc(q_std, 1)

            act.wait_ge(cst_in_sem, 32)
            act.wait_ge(dve_setup, 2)
            activation(LG[:, 32:48], LG[:, 16:32], ACT.Exp).then_inc(act_setup, 1)
            act.wait_ge(dve_setup, 3)
            activation(LG[:, 56:64], LG[:, 48:56], ACT.Ln).then_inc(act_setup, 1)

            def layer(l, last):
                norm(l, norms[0], 0)
                ffn(l, 0)
                norm(l, norms[1], 1)
                project_hg(l)
                gla(l, last)
                project_rw(l)
                rwkv_prep(l)
                rwkv(l)
                y_post(l, last)
                norm(l, norms[2], 2, last)
                ffn(l, 1, last)

            act.wait_ge(x_loaded, 16)
            condition(1)
            with act.Fori(0, DEPTH - 1) as l:
                layer(l, False)
            layer(DEPTH - 1, True)
            norm(0, fnorm, None, True)

        @block.vector
        def _(dve):
            tt, ts, stt = (ordered(dve, f) for f in (dve.tensor_tensor, dve.tensor_scalar, dve.scalar_tensor_tensor))
            tensor_copy, memset, reciprocal, copy_predicated, tensor_tensor_scan, tensor_tensor_reduce = (
                ordered(dve, f) for f in (dve.tensor_copy, dve.memset, dve.reciprocal, dve.copy_predicated,
                                          dve.tensor_tensor_scan, dve.tensor_tensor_reduce))

            def square(x, sp):
                tt(TM[:, 3, sp], x, x, ALU.mult)
                return tt(TM[:, 2, sp], TM[:, 2, sp], TM[:, 3, sp], ALU.add)

            def norm(l, s, n, lat=False):
                for a, (sl, _) in enumerate(halves(0, lat)):
                    dve.wait_ge(s.std_ready, (1 if lat and n is None else l * 2 + (a + 1)))
                    reciprocal(TM[:, 3, sl], TM[:, 3, sl])
                for k in range(KT):
                    for sl, _ in halves(0, lat):
                        q = 1 if sl.start == 0 else 0
                        gain = CST[:, C_FG + k:C_FG + k + 1] if n is None else coef[:, n, 0, k, q:q + 1]
                        last = stt(H[:, k, sl], X[:, k, sl], gain, TM[:, 3, sl], ALU.mult, ALU.mult)
                    last.then_inc(s.h_ready if n is None else s.x_scaled, 1)
                if n in (0, 2):
                    for k in range(KT):
                        dve.wait_ge(s.h_ready, l * KT + k + 1)
                        stt(HL[:, k], H[:, k, CTX:T], coef[:, n, 1, k, 0:1], HH[:, k].bitcast(F32), ALU.add,
                            ALU.subtract).then_inc(s.low_ready, 1)

            def residual(l, n, first, slots, done, lat, summed, mod=None):
                memset(TM[:, 2], 0.0)
                with dve.Fori(0, 2) as g:
                    if mod is not None:
                        for a in range(2):
                            modulation(mod[0], g * 2 + (mod[1] + a))
                    for m in range(4):
                        dve.wait_ge(w_used, l * SLOTS + g * (4 * slots) + (first + slots * (m + 1)))
                        xk = X[:, bass.ds(g * 4 + m, 1)].rearrange("p a t -> p (a t)")
                        ck = coef[:, n, 2, bass.ds(g * 4 + m, 1)].rearrange("p a s -> p (a s)")
                        for sl, src in halves(2 * m, lat):
                            q = 1 if sl.start == 0 else 0
                            last = stt(xk[:, sl], src, ck[:, q:q + 1], xk[:, sl], ALU.mult, ALU.add)
                        last.then_inc(done, 1)
                        square(xk[:, span(lat)], span(lat))
                dve.nop().then_inc(summed, 1)

            def ffn(l, n, summed, lat=False):
                s = ffns[n]

                def hidden(i):
                    for j in range(2):
                        dve.wait_ge(s.silu_done, l * FT + i * 2 + (j + 1))
                        dst = A[:, bass.ds(i * 2 + j, 1)].rearrange("p a t -> p (a t)")
                        for sl, src in halves(4 * j + 2, lat):
                            last = tt(dst[:, sl], TM[:, j, sl], src, ALU.mult)
                        last.then_inc(s.act_done, 1)

                with dve.Fori(0, FT // 2) as i:
                    hidden(i)
                mod = None
                if not lat:
                    dve.wait_ge(cvec_ready, l * 2 + n + 2)
                    settle(dve, "dve")
                    if n == 0:
                        with dve.Fori(MG_NEXT, MG_GATE) as i:
                            modulation(l, i)
                        gate_coefficient(0)
                        mod = (l, MG_GATE)
                    else:
                        dve.wait_ge(par_loaded, 32 * (l + 2))
                        settle(dve, "dve")
                        mod = (l + 1, 0)
                residual(l, 2 * n, (S_DN1, S_DN2)[n], 3, s.res_done, lat, summed, mod)
                if not lat:
                    shift_scale(1 - n)

            def modulation(l, i):
                bm = PAR[:, COLS["b_mod"][0]:COLS["b_mod"][1]]
                for j in range(RING):
                    dve.wait_ge(m_ready[j], (l * MG + i + 1) * 16)
                    for q in range(2):
                        last = tensor_tensor_reduce(JUNK, WM[j], CBC[:, q], 1.0, 0.0, ALU.mult, ALU.add,
                                                    MTMP[:, 2 * j + q:2 * j + q + 1])
                    last.then_inc(m_used, 1)
                tt(MOD[:, bass.ds(i * 2 * RING, 2 * RING)].rearrange("p (k s) -> p k s", s=2),
                   MTMP[:, :].rearrange("p (k s) -> p k s", s=2),
                   bm[:, bass.ds(i * RING, RING)].unsqueeze(2).to_broadcast([P, RING, 2]), ALU.add)

            def shift_scale(n):
                g = par("gain", n * KT, KT).unsqueeze(2).to_broadcast([P, KT, 2])
                stt(coef[:, n, 0], modv[:, 3 * n + 1], 1.0, g, ALU.add, ALU.mult)
                tensor_copy(coef[:, n, 1], modv[:, 3 * n])

            def gate_coefficient(n):
                ts(coef[:, n, 2], modv[:, 3 * n + 2], 1.0 if n == 1 else 0.5, None, ALU.mult)

            def gla(l, lat):
                dve.wait_ge(hg_silu, l + 1)
                dve.wait_ge(spilled, 16 * (l + 1))
                settle(dve, "dve")

                def bounds(h):
                    lbl = LBC[:, bass.ds(l * 16 + h, 13)]
                    tensor_copy(LBH[:, :], lbl[:, 0:13:4]).then_inc(g_lb, 1)

                def gate_sum(v, d):
                    dve.wait_ge(g_f, v + 1)
                    for c in range(GN):
                        sl = slice(c * GC, (c + 1) * GC)
                        o, src = G_B[d][:, sl], G_RB[:, sl]
                        if d == 1:
                            o, src = o[:, ::-1], src[:, ::-1]
                        last = tensor_tensor_scan(o, ones, src, 0.0, ALU.mult, ALU.add)
                    last.then_inc(g_b, 1)

                def unit(h, d, nxt):
                    v = (l * HT + h) * 2 + d

                    def sides(t, m):
                        w = t.rearrange("p (b s m) -> p b s m", s=2, m=m)
                        return w[:, :, 1 - d], w[:, :, d]

                    def exponents(n):
                        m = LEVELS[n]
                        bq, bk = sides(G_B[d], m)
                        eq, ek = sides(G_E[n % 2], m)
                        at_ = 0 if d else m - 1
                        ref = bk[:, :, at_:at_ + 1].to_broadcast([P, T // (2 * m), m])
                        dve.tensor_tensor(eq, bq, ref, ALU.subtract)
                        tt(ek, ref, bk, ALU.subtract).then_inc(g_dx, 1)

                    def scale(n):
                        m = LEVELS[n]
                        dve.wait_ge(g_ex, v * 7 + (n + 1))
                        if n >= 2:
                            dve.wait_ge(g_att_ps, v * 8 + n)
                        eq, ek = sides(G_E[n % 2], m)
                        zq, zk = sides(G_Z[n % 2], m)
                        dve.tensor_tensor(zq, eq, sides(G_QS[d], m)[0], ALU.mult)
                        tt(zk, ek, sides(G_KS[d], m)[1], ALU.mult).then_inc(g_z, 1)

                    def merge(n):
                        dve.wait_ge(g_att_ps, v * 8 + (n + 2))
                        settle(dve, "dve")
                        b = 2 * ((n + 1) % 2)
                        o = C_LVL + (d * len(LEVELS) + n) * P
                        for a in range(2):
                            mask = CST[:, o:o + P].bitcast(U32).unsqueeze(1).to_broadcast([P, 3, GC])
                            last = copy_predicated(chunked(G_ATT[d])[:, 3 * a:3 * a + 3], mask,
                                                   ps[:, b + a, 0:384].rearrange("p (c t) -> p c t", t=GC))
                        last.then_inc(g_att, 1)

                    dve.wait_ge(g_k, v + 1)
                    settle(dve, "dve")
                    if nxt is not None and nxt[1] == 0:
                        bounds(nxt[0])
                    exponents(0)
                    dve.wait_ge(g_att_ps, v * 8 + 1)
                    for a in range(2):
                        last = tt(chunked(G_ATT[d])[:, 3 * a:3 * a + 3],
                                  ps[:, a, 0:384].rearrange("p (c t) -> p c t", t=GC),
                                  ident.unsqueeze(1).to_broadcast([P, 3, GC]), ALU.mult)
                    last.then_inc(g_att, 1)
                    for n in range(len(LEVELS)):
                        if n + 1 < len(LEVELS):
                            exponents(n + 1)
                        scale(n)
                        if n >= 1:
                            merge(n - 1)
                        if n == 2:
                            dve.wait_ge(g_u, v + 1)
                            order = GLA_ORDER[d]
                            for a, c in enumerate(order[:-1]):
                                nc_ = order[a + 1]
                                dst = G_S[d][:, nc_ * GC:(nc_ + 1) * GC]
                                src = ps[:, 4 + c // 3, (c % 3) * GC:(c % 3 + 1) * GC]
                                if a == 0:
                                    last = tensor_copy(dst, src)
                                else:
                                    last = stt(dst, G_S[d][:, c * GC:(c + 1) * GC], EBL[d][:, c:c + 1], src,
                                               ALU.mult, ALU.add)
                            last.then_inc(g_s, 1)
                        if nxt is not None and n == 4:
                            gate_sum(v + 1, nxt[1])
                    merge(len(LEVELS) - 1)

                bounds(0)
                gate_sum(l * HT * 2, 0)
                with dve.Fori(0, HT - 1) as h:
                    unit(h, 0, (h, 1))
                    unit(h, 1, (h + 1, 0))
                unit(HT - 1, 0, (HT - 1, 1))
                unit(HT - 1, 1, None)
                for h in range(HT):
                    dve.wait_ge(on_std, l * HT + h + 1)
                    sp = span(lat)
                    reciprocal(xt(h)[:, sp], xt(h)[:, sp]).then_inc(on_rec, 1)

            def convolve(l):
                def group(i, k):
                    for j in range(k):
                        dve.wait_ge(rw_ev, l * RW_T + i * RING + (j + 1) + 4)
                        src = TM[:, j % 2]
                        dst = A[:, bass.ds(i * RING + j, 1)].rearrange("p a t -> p (a t)")
                        a0 = COLS["taps"][0]
                        taps = PAR[:, a0:a0 + RW_T * 9][:, bass.ds((i * RING + j) * 9, 9)]
                        ts(dst, src, taps[:, 4:5], None, ALU.mult)
                        stt(dst[:, 1:CTX], src[:, 0:CTX - 1], taps[:, 3:4], dst[:, 1:CTX], ALU.mult, ALU.add)
                        stt(dst[:, 0:CTX - 1], src[:, 1:CTX], taps[:, 5:6], dst[:, 0:CTX - 1], ALU.mult, ALU.add)
                        sg = src[:, CTX:T].rearrange("p (y x) -> p y x", x=GRID_W)
                        dg = dst[:, CTX:T].rearrange("p (y x) -> p y x", x=GRID_W)
                        for dy in (-1, 0, 1):
                            for dx in (-1, 0, 1):
                                if dy == 0 and dx == 0:
                                    continue
                                y0, y1 = max(0, -dy), GRID_H - max(0, dy)
                                x0, x1 = max(0, -dx), GRID_W - max(0, dx)
                                n = (dy + 1) * 3 + dx + 1
                                o = dg[:, y0:y1, x0:x1]
                                last = stt(o, sg[:, y0 + dy:y1 + dy, x0 + dx:x1 + dx], taps[:, n:n + 1], o,
                                           ALU.mult, ALU.add)
                        last.then_inc(rw_conv, 1)
                with dve.Fori(0, RW_T // RING) as i:
                    group(i, RING)
                group(RW_T // RING, RW_T % RING)

            def rwkv_prep(l):
                dve.wait_ge(on_done, l + 1)
                settle(dve, "dve")
                for j in range(HT):
                    ts(R_kk[:, j], R_k[:, j], par("k_k", j), None, ALU.mult)
                    tt(TM[:, j], R_kk[:, j], R_kk[:, j], ALU.mult).then_inc(p_sq, 1)
                for j in range(HT):
                    dve.wait_ge(p_ss, l * HT + j + 1)
                    for sl, src in halves(2 * j):
                        last = ts(TM[:, j, sl], src, 1e-24, None, ALU.max)
                    last.then_inc(p_mx, 1)
                for j in range(HT):
                    dve.wait_ge(p_sd, l * HT + j + 1)
                    reciprocal(TM[:, j], TM[:, j])
                    tt(R_kk[:, j], R_kk[:, j], TM[:, j], ALU.mult).then_inc(p_kn, 1)
                for z in (R_STF, YB, R_AKK, R_UI):
                    memset(z, 0.0)
                for d in range(2):
                    hf = slice(64 * d, 64 * d + 64)
                    tensor_copy(R_UI[hf, :, hf], ident[hf, hf].unsqueeze(1).to_broadcast([64, 8, 64]))
                dve.wait_ge(o_spilled, 16 * (l + 1))
                dve.wait_ge(p_ev, l * 16 + 16 + 4)
                settle(dve, "dve")
                memset(R_EP[:, 0, :, 0:1], 1.0)
                memset(R_EP[:, 1, :, RC:RC + 1], 1.0)

            def rwkv(l):
                hd = [slice(0, 64), slice(64, 128)]
                ka = par("k_a", 0, HT).unsqueeze(2).to_broadcast([P, HT, RC])
                oka = KAX[:, 0:HT].unsqueeze(2).to_broadcast([P, HT, RC])
                bs, ks = (0, 1), (1, 0)

                def chunk(t, c):
                    return t[:, :, bass.ds(c * RC, RC)]

                def cumulate(c):
                    tensor_copy(R_EI[:, 1], chunk(R_lw[1], c[1]))
                    for j in range(HT):
                        tensor_tensor_scan(R_T1[:, 0, j], ones[:, 0:RC], chunk(R_lw[0], c[0])[:, j], 0.0,
                                           ALU.mult, ALU.add)
                        last = tensor_tensor_scan(R_T1[:, 1, j, ::-1], ones[:, 0:RC], R_EI[:, 1, j, ::-1], 0.0,
                                                  ALU.mult, ALU.add)
                    last.then_inc(r_cum, 1)

                def scale_bk(c, d, part):
                    if part == 0:
                        tt(R_BK[:, d, :, bs[d]], chunk(R_kk, c[d]), chunk(R_a[d], c[d]), ALU.mult)
                        tt(R_BK[:, d, :, ks[d]], chunk(R_a[d], c[d]), ka, ALU.mult)
                        tt(R_BK[:, d, :, bs[d]], R_BK[:, d, :, bs[d]], R_EI[:, d], ALU.mult)
                        tensor_copy(R_T1[:, d], chunk(R_v, c[d]))
                    else:
                        tt(R_BK[:, d, :, ks[d]], R_BK[:, d, :, ks[d]], oka, ALU.add)
                        tt(R_BK[:, d, :, ks[d]], R_BK[:, d, :, ks[d]], chunk(R_k, c[d]), ALU.mult)
                        last = tt(R_BK[:, d, :, ks[d]], R_BK[:, d, :, ks[d]], R_EI[:, d], ALU.mult)
                        if d == 1:
                            last.then_inc(r_bk, 1)

                def scale_kr(c, d):
                    prev, here = (0, 1) if d == 0 else (1, 0)
                    tt(R_KR[:, d, :, 0], chunk(R_kk, c[d]), R_EP[:, d, :, prev:prev + RC], ALU.mult)
                    last = tt(R_KR[:, d, :, 1], chunk(R_r, c[d]), R_EP[:, d, :, here:here + RC], ALU.mult)
                    if d == 1:
                        last.then_inc(r_kr, 1)

                def am(d):
                    return ps[:, 2 * d:2 * d + 2, :].rearrange("p e (j c) -> p e j c", j=HT)

                def mask_kk(u):
                    dve.wait_ge(r_am_ps, u + 1)
                    settle(dve, "dve")
                    strict = [CST[:, C_AM + d * P:C_AM + d * P + 64] for d in range(2)]
                    for d in range(2):
                        for e in range(2):
                            copy_predicated(R_UI[hd[d], e:8:2, hd[d]],
                                            strict[d][hd[d]].bitcast(U32).unsqueeze(1).to_broadcast([64, HT, 64]),
                                            am(d)[hd[d], e, :, 0:64])
                            q = hd[1 - d]
                            tt(R_AKK[q, e:8:2, hd[d]], am(d)[q, e, :, 0:64],
                               strict[d][q].unsqueeze(1).to_broadcast([64, HT, 64]), ALU.mult)

                def mask_r():
                    for d in range(2):
                        incl = CST[:, C_AM + d * P + 64:C_AM + (d + 1) * P].unsqueeze(1).to_broadcast([P, HT, 64])
                        for e in range(2):
                            last = tt(R_AMR[:, d, e:8:2], am(d)[:, e, :, 64:128], incl, ALU.mult)
                    last.then_inc(r_am, 1)

                def step(u, c, nxt):
                    for d, end in ((0, RC), (1, 0)):
                        tensor_copy(PCT[:, d * HT:(d + 1) * HT].unsqueeze(2), R_EP[:, d, :, end:end + 1])
                    for n in range(len(INV)):
                        o = C_INV + n * P
                        m = CST[:, o:o + P].unsqueeze(1).to_broadcast([P, 4, P])
                        for g in range(2):
                            q = slice(4 * g, 4 * g + 4)
                            if n == 0:
                                tt(R_Y[:, q], R_UI[:, q],
                                   CST[:, C_INV0T:C_INV0T + P].unsqueeze(1).to_broadcast([P, 4, P]), ALU.mult)
                            dve.wait_ge(r_t, u * 12 + (2 * n + g + 1))
                            tt((R_X if n == 0 else R_W)[:, q], ps[:, g, :].rearrange("p (h c) -> p h c", h=4), m,
                               ALU.mult).then_inc(r_w, 1)
                        if nxt is not None:
                            if n == 0:
                                cumulate(nxt)
                            if n == 2:
                                dve.wait_ge(r_exp, u + 2)
                            if n in (2, 3):
                                scale_bk(nxt, n - 2, 0)
                                scale_bk(nxt, n - 2, 1)
                            if n == 4:
                                scale_kr(nxt, 0)
                                scale_kr(nxt, 1)
                    if nxt is not None:
                        mask_kk(u + 1)
                    dve.wait_ge(r_s, u + 1)
                    for e in range(2):
                        q = hd[e]
                        st = R_STF[q].rearrange("p (g c) -> p g c", c=P)[:, :, hd[e]]
                        tt(st, st, ps[q, 6, :].rearrange("p (g c) -> p g c", c=64), ALU.add)
                        last = tt(st, st, PCT[q].unsqueeze(2).to_broadcast([64, 2 * HT, 64]), ALU.mult)
                    last.then_inc(r_se, 1)
                    dve.wait_ge(r_y, u + 1)
                    if nxt is not None:
                        mask_r()
                    for d in range(2):
                        y = chunk(YB, c[d])
                        last = tt(y, y, ps[:, 7, d * 256:(d + 1) * 256].rearrange("p (j c) -> p j c", j=HT), ALU.add)
                    last.then_inc(r_ye, 1)

                def pair(i, mirror):
                    return (i, mirror - i)

                u0 = l * RN
                m_ctx, m_lat = RN_CTX - 1, RN + RN_CTX - 1
                first = pair(0, m_ctx)
                cumulate(first)
                dve.wait_ge(r_exp, u0 + 1)
                for d in range(2):
                    for part in range(2):
                        scale_bk(first, d, part)
                for d in range(2):
                    scale_kr(first, d)
                mask_kk(u0)
                mask_r()
                with dve.Fori(0, RN_CTX - 1) as i:
                    step(u0 + i, pair(i, m_ctx), pair(i + 1, m_ctx))
                step(u0 + (RN_CTX - 1), pair(RN_CTX - 1, m_ctx), pair(RN_CTX, m_lat))
                with dve.Fori(RN_CTX, RN - 1) as i:
                    step(u0 + i, pair(i, m_lat), pair(i + 1, m_lat))
                step(u0 + (RN - 1), pair(RN - 1, m_lat), None)

            def y_post(l, lat):
                sp = span(lat)

                def bonus(j):
                    b = Y_BONUS[j][:, sp]
                    tt(b, R_a[0][:, j, sp], R_a[1][:, j, sp], ALU.add)
                    ts(b, b, par("k_a", j), KAX[:, HT + j:HT + j + 1], ALU.mult, ALU.add)
                    tt(b, b, R_k[:, j, sp], ALU.mult)
                    stt(b, b, par("r_k", j), R_r[:, j, sp], ALU.mult, ALU.mult).then_inc(q_a, 1)

                bonus(0)
                for j in range(HT):
                    dve.wait_ge(q_b, l * HT + j + 1)
                    for sl, src in halves(2 * j, lat):
                        last = stt(YB[:, j, sl], src, -1.0 / 64, YB[:, j, sl], ALU.mult, ALU.add)
                    last.then_inc(q_e, 1)
                for j in range(1, HT):
                    bonus(j)
                for j in range(HT):
                    y = YB[:, j, sp]
                    dve.wait_ge(q_std, l * HT + j + 1)
                    reciprocal(TM[:, j, sp], TM[:, j, sp])
                    stt(y, y, par("ln_w", j), TM[:, j, sp], ALU.mult, ALU.mult)
                    dve.wait_ge(q_v, l * HT + j + 1)
                    for sl, src in halves(2 * j, lat):
                        last = tt(Y_BONUS[j][:, sl], R_v[:, j, sl], src, ALU.mult)
                    last.then_inc(q_ve, 1)
                    stt(y, y, par("ln_b", j), Y_BONUS[j][:, sp], ALU.add, ALU.add)
                for j in range(HT):
                    dve.wait_ge(q_g, l * HT + j + 1)
                    for sl, src in halves(2 * j, lat):
                        last = tt(YB[:, j, sl], YB[:, j, sl], src, ALU.mult)
                    last.then_inc(q_f, 1)

            dve.wait_ge(cst_in_sem, 32)
            for s, n in ([(f.act_done, 2) for f in ffns] + [(f.res_done, 4) for f in ffns] +
                         [(m_used, RING), (wc_used, 2), (hg_ev, 4), (rw_ev, 4), (rw_conv, 2), (out_res, 4), (p_ev, 4),
                          (r_se, 1), (r_ye, 1)]):
                dve.nop().then_inc(s, n)
            memset(EPS[:, 0:1], RMS_EPS)
            memset(EPS[:, 1:2], GN_EPS)
            dve.nop().then_inc(dve_setup, 1)
            tt(LG[:, 48:56], LG[:, 0:8], LG[:, 8:16], ALU.max)
            tt(LG[:, 16:24], LG[:, 0:8], LG[:, 48:56], ALU.subtract)
            tt(LG[:, 24:32], LG[:, 8:16], LG[:, 48:56], ALU.subtract).then_inc(dve_setup, 1)
            dve.wait_ge(act_setup, 1)
            tt(LG[:, 48:56], LG[:, 32:40], LG[:, 40:48], ALU.add).then_inc(dve_setup, 1)
            dve.wait_ge(act_setup, 2)
            memset(LBC[:, 0:8], NEVER)
            memset(LBC[:, 8:16], 1.0)
            tt(LBC[:, 16:24], LG[:, 24:32], LG[:, 56:64], ALU.subtract)
            reciprocal(LG[:, 48:56], LG[:, 48:56])
            tt(LBC[:, 24:32], LG[:, 32:40], LG[:, 48:56], ALU.mult)

            def layer(l, last):
                norm(l, norms[0], 0)
                ffn(l, 0, norms[1].sum_ready)
                norm(l, norms[1], 1)
                with dve.Fori(MG_FFN, MG) as i:
                    modulation(l, i)
                gate_coefficient(1)
                shift_scale(2)
                gate_coefficient(2)
                ts(KAX[:, 0:HT], par("k_a", 0, HT), -1.0, 1.0, ALU.mult, ALU.add)
                ts(KAX[:, HT:], par("k_a", 0, HT), -2.0, 2.0, ALU.mult, ALU.add)
                gla(l, last)
                convolve(l)
                rwkv_prep(l)
                rwkv(l)
                dve.nop().then_inc(xr_free, 1)
                y_post(l, last)
                dve.nop().then_inc(par_free, 1)
                dve.wait_ge(reloaded, 32 * (l + 1))
                settle(dve, "dve")
                residual(l, 1, S_OUT, 1, out_res, last, norms[2].sum_ready)
                norm(l, norms[2], 2, last)
                ffn(l, 1, fnorm.sum_ready if last else norms[0].sum_ready, last)

            dve.wait_ge(x_loaded, 16)
            memset(TM[:, 2], 0.0)
            for k in range(KT):
                last = square(X[:, k], span(False))
            last.then_inc(norms[0].sum_ready, 1)
            dve.wait_ge(cvec_ready, 1)
            dve.wait_ge(par_loaded, 32)
            with dve.Fori(0, MG_NEXT) as i:
                modulation(0, i)
            shift_scale(0)
            with dve.Fori(0, DEPTH - 1) as l:
                layer(l, False)
            layer(DEPTH - 1, True)
            norm(0, fnorm, None, True)


def constants(np):
    c = np.zeros((P, NCST), np.float32)
    c[:, C_ID:C_ID + P] = np.eye(P)
    c[:, C_ONE:C_ONE + P] = 1.0
    c[:64, C_BLK:C_BLK + 64] = 1.0
    c[64:, C_BLK + 64:C_BLK + P] = 1.0
    s, t = np.arange(GC)[:, None], np.arange(GC)[None, :]
    for n, m in enumerate(LEVELS):
        fw = (s // (2 * m) == t // (2 * m)) & (s // m % 2 == 0) & (t // m % 2 == 1)
        c[:, C_LVL + n * P:C_LVL + (n + 1) * P] = fw
        c[:, C_LVL + (len(LEVELS) + n) * P:C_LVL + (len(LEVELS) + n + 1) * P] = fw.T
    i, t = np.arange(RC)[:, None], np.arange(RC)[None, :]
    fw = np.concatenate([i < t, i <= t], axis=1)
    bw = np.concatenate([i > t, i >= t], axis=1)
    c[:, C_AM:C_AM + P] = np.concatenate([fw, fw])
    c[:, C_AM + P:C_AM + 2 * P] = np.concatenate([bw, bw])
    for n, m in enumerate(INV):
        fw = (i // (2 * m) == t // (2 * m)) & (i // m % 2 == 0) & (t // m % 2 == 1)
        lvl = np.eye(P, dtype=np.float32)
        lvl[:64, :64] -= fw.T
        lvl[64:, 64:] -= fw
        c[:, C_INV + n * P:C_INV + (n + 1) * P] = lvl
        if n == 0:
            c[:, C_INV0T:C_INV0T + P] = lvl.T
    return c


def kernel(**inputs):
    import numpy as np
    import concourse.bacc as bacc
    from concourse.bass_utils import run_bass_kernel_spmd

    v = {k: np.asarray(a) for k, a in inputs.items()}

    def by_tile(a):
        return np.moveaxis(a.reshape(-1, P), 0, 1)

    def columns(w):
        k, m = w.shape
        return w.reshape(k // P, P, m // P, P).transpose(2, 1, 0, 3).reshape(m // P, P, -1)

    stream = np.zeros((DEPTH * SLOTS, P, 1024), np.float32)
    mods = np.zeros((DEPTH * MT, P, D), np.float32)
    par_a = np.zeros((DEPTH, P, NPAR), np.float32)
    small = np.zeros((DEPTH, P, 3 * 512), np.float32)
    for l in range(DEPTH):
        s = stream[l * SLOTS:(l + 1) * SLOTS]
        mods[l * MT:(l + 1) * MT] = v["w_mod"][l].T.reshape(MT, P, D)
        for n, (up, dn) in enumerate(((S_UP1, S_DN1), (S_UP2, S_DN2))):
            w = columns(v[f"ffn{n + 1}_up"][l])
            s[up:up + 2 * FT:2] = w[:FT]
            s[up + 1:up + 2 * FT:2] = w[FT:]
            w = columns(v[f"ffn{n + 1}_down"][l])
            k0 = 0
            for r, nk in enumerate(DOWN_K):
                s[dn + r:dn + 3 * KT:3, :, 0:nk * P] = w[:, :, k0 * P:(k0 + nk) * P]
                k0 += nk
        w = columns(v["w_in"][l])
        s[S_HG:S_HG + HG_T] = w[:HG_T]
        s[S_RW:S_RW + RW_T] = w[HG_T:]
        s[S_OUT:S_OUT + KT] = columns(v["w_out"][l])
        for name, a in (("gain", by_tile(v["norm_gains"][l])), ("ogain", by_tile(v["hgrn_o_gain"][l])),
                        ("taps", v["rwkv_conv"][l].reshape(9, RW_T, P).transpose(2, 1, 0).reshape(P, -1)),
                        ("w0", by_tile(v["rwkv_w0"][l])), ("a0", by_tile(v["rwkv_a0"][l])),
                        ("k_k", by_tile(v["rwkv_k_k"][l])), ("k_a", by_tile(v["rwkv_k_a"][l])),
                        ("r_k", by_tile(v["rwkv_r_k"][l])), ("ln_w", by_tile(v["rwkv_ln_w"][l])),
                        ("ln_b", by_tile(v["rwkv_ln_b"][l])), ("b_mod", by_tile(v["b_mod"][l]))):
            a0, a1 = COLS[name]
            par_a[l, :, a0:a1] = a
        small[l, :, 0:512] = v["rwkv_w_up"][l].reshape(P, 512)
        small[l, :, 512:1024] = v["rwkv_a_up"][l].reshape(P, 512)
        small[l, :, 1024:] = v["rwkv_g_up"][l]
    cst = constants(np)
    cst[:, C_FG:C_FG + KT] = by_tile(v["final_gain"])
    tokens = np.concatenate([v["ctx"][0], v["x"][0]])
    x_in = np.ascontiguousarray(tokens.T.reshape(KT, P, T).transpose(1, 0, 2))
    cvec = np.ascontiguousarray(np.broadcast_to(np.concatenate([v["c"][0], v["c_ctx"]])[None], (P, 2 * D)))
    arrays = {"x_in": x_in, "wstream": stream, "mstream": mods, "par_in": par_a, "small_in": small, "cst_in": cst,
              "logit_in": np.ascontiguousarray(by_tile(v["hgrn_lb_logits"])), "cvec_in": cvec}

    nc = bacc.Bacc("TRN2", target_bir_lowering=False, num_devices=1)
    args = [nc.dram_tensor(n, a.shape, F32, kind="ExternalInput").ap() for n, a in arrays.items()]
    out = nc.dram_tensor("out", (P, KT, LAT), F32, kind="ExternalOutput").ap()
    build_program(nc, *args, out)
    r = run_bass_kernel_spmd(nc, [arrays], core_ids=[0])
    got = r.results[0]["out"]
    return np.ascontiguousarray(got.transpose(2, 1, 0).reshape(1, LAT, D))
```
